# Optimizing a Trainium2 kernel written in Bass

```python
import jax, jax.numpy as jnp
from jax import lax
import numpy as np

D_MODEL = 1024
BATCH = 1
SEQ = 512
DEPTH = 2

GRID_W = 64
CTX_LEN = 256
N_MOD = 9
D_FF = 2752
EPS = 1e-6
ATTN_HEADS = 4
Q_LORA = 256
KV_LORA = 128
NOPE_DIM = 128
ROPE_DIM = 64
AXIS_FREQS = ROPE_DIM // 4
V_DIM = 128
ATTN_WIDTH = ATTN_HEADS * V_DIM
ROPE_BASE = 10000.0
SM_SCALE = (NOPE_DIM + ROPE_DIM) ** -0.5
Q_BLOCK = 128
MLSTM_HEADS = 4
MLSTM_DH = 128
MLSTM_WIDTH = MLSTM_HEADS * MLSTM_DH
MLSTM_CHUNK = 64
CONV_K = 3
N_GATES = 4 * MLSTM_HEADS
IN_SIZES = (Q_LORA, KV_LORA, ROPE_DIM, 2 * MLSTM_WIDTH, MLSTM_WIDTH, MLSTM_WIDTH, N_GATES)
D_IN = Q_LORA + KV_LORA + ROPE_DIM + 4 * MLSTM_WIDTH + N_GATES
MIX_WIDTH = ATTN_WIDTH + MLSTM_WIDTH

kernel_name = 'hybrid_mla_mlstm_dit_block'

def rms_norm(x, g):
    xf = x.astype(jnp.float32)
    y = xf * lax.rsqrt(jnp.mean(xf * xf, axis=-1, keepdims=True) + EPS)
    return (y * g.astype(jnp.float32)).astype(x.dtype)

def head_layer_norm(h, g):
    mu = jnp.mean(h, axis=-1, keepdims=True)
    var = jnp.mean(jnp.square(h - mu), axis=-1, keepdims=True)
    y = (h - mu) * lax.rsqrt(var + EPS)
    return y.reshape(h.shape[:2] + (-1,)) * g.astype(jnp.float32)

def swiglu(h, wg, wu, wd):
    return (jax.nn.silu(h @ wg) * (h @ wu)) @ wd

def split_in(p):
    offs = [int(o) for o in np.cumsum(IN_SIZES)[:-1]]
    return jnp.split(p, offs, axis=-1)

def conv_centred(u, w, b):
    pad = CONV_K // 2
    t = u.shape[1]
    up = jnp.pad(u, ((0, 0), (pad, pad), (0, 0)))
    out = up[:, 0:t] * w[0]
    for j in range(1, CONV_K):
        out = out + up[:, j:j + t] * w[j]
    return out + b

def axial_rope_tables(n_tokens):
    rows = n_tokens // GRID_W
    t_row = jnp.repeat(jnp.arange(rows), GRID_W).astype(jnp.float32)
    t_col = jnp.tile(jnp.arange(GRID_W), rows).astype(jnp.float32)
    inv = ROPE_BASE ** (-jnp.arange(AXIS_FREQS, dtype=jnp.float32) / AXIS_FREQS)
    ang = jnp.stack([t_row[:, None] * inv, t_col[:, None] * inv], axis=1)
    return jnp.cos(ang)[:, None], jnp.sin(ang)[:, None]

def apply_axial_rope(x, cos, sin):
    sh = x.shape
    xr = x.reshape(sh[:-1] + (2, 2, AXIS_FREQS))
    x1, x2 = xr[..., 0, :], xr[..., 1, :]
    cos = cos.astype(x.dtype)
    sin = sin.astype(x.dtype)
    out = jnp.stack([x1 * cos - x2 * sin, x2 * cos + x1 * sin], axis=-2)
    return out.reshape(sh)

def mla_query(cq, q_norm, w_uq):
    b, t, _ = cq.shape
    return (rms_norm(cq, q_norm) @ w_uq).reshape(b, t, ATTN_HEADS, NOPE_DIM + ROPE_DIM)

def mla_keys(ckv, k_rope, kv_norm, w_ukv):
    b, t, _ = ckv.shape
    kv = (rms_norm(ckv, kv_norm) @ w_ukv).reshape(b, t, ATTN_HEADS, NOPE_DIM + V_DIM)
    k = jnp.concatenate([kv[..., :NOPE_DIM],
                         jnp.broadcast_to(k_rope, (b, t, ATTN_HEADS, ROPE_DIM)).astype(kv.dtype)], axis=-1)
    return k, kv[..., NOPE_DIM:]

def softmax_attend(q, k, v):
    s = jnp.einsum('bqhd,bkhd->bhqk', q, k).astype(jnp.float32) * SM_SCALE
    p = jax.nn.softmax(s, axis=-1).astype(v.dtype)
    return jnp.einsum('bhqk,bkhd->bqhd', p, v)

def blocked_attention(q, k, v):
    b, s, h, dk = q.shape
    nb = s // Q_BLOCK
    qb = jnp.swapaxes(q.reshape(b, nb, Q_BLOCK, h, dk), 0, 1)
    ob = lax.map(lambda qq: softmax_attend(qq, k, v), qb)
    return jnp.swapaxes(ob, 0, 1).reshape(b, s, h * v.shape[-1])

def mlstm_state_update(state, k, v, ig, b):
    C, n, m = state
    b_last = b[..., -1]
    log_w = b_last[..., None] - b + ig
    m_new = jnp.maximum(b_last + m, jnp.max(log_w, axis=-1))
    w = jnp.exp(log_w - m_new[..., None])
    decay = jnp.exp(b_last + m - m_new)
    C = decay[..., None, None] * C + jnp.einsum('bhsd,bhse->bhde', w[..., None] * k, v)
    n = decay[..., None] * n + jnp.einsum('bhs,bhsd->bhd', w, k)
    return (C, n, m_new)

def mlstm_chunkwise(q, k, v, ig, lf, state):
    bq, h, t, dh = q.shape
    nc = t // MLSTM_CHUNK
    tri = jnp.tril(jnp.ones((MLSTM_CHUNK, MLSTM_CHUNK), dtype=bool))

    def chunks(a):
        a = a.reshape((bq, h, nc, MLSTM_CHUNK) + a.shape[3:])
        return jnp.moveaxis(a, 2, 0)

    def step(carry, inp):
        C, n, m = carry
        qc, kc, vc, igc, lfc = inp
        b = jnp.cumsum(lfc, axis=-1)
        log_d = jnp.where(tri, b[..., :, None] - b[..., None, :] + igc[..., None, :], -jnp.inf)
        log_inter = b + m[..., None]
        m_t = jnp.maximum(log_inter, jnp.max(log_d, axis=-1))
        s = jnp.einsum('bhtd,bhsd->bhts', qc, kc) * jnp.exp(log_d - m_t[..., None])
        inter = jnp.exp(log_inter - m_t)
        num = jnp.einsum('bhts,bhsd->bhtd', s, vc) + inter[..., None] * jnp.einsum('bhtd,bhde->bhte', qc, C)
        den = jnp.sum(s, axis=-1) + inter * jnp.einsum('bhtd,bhd->bht', qc, n)
        hc = num / jnp.maximum(jnp.abs(den), jnp.exp(-m_t))[..., None]
        return mlstm_state_update(carry, kc, vc, igc, b), hc

    state, hs = lax.scan(step, state, (chunks(q), chunks(k), chunks(v), chunks(ig), chunks(lf)))
    return jnp.moveaxis(hs, 0, 2).reshape(bq, h, t, dh), state

def mlstm_inputs(qk_pre, v, gates, conv_w, conv_b, gate_b):
    b, t, _ = v.shape
    u = jax.nn.silu(conv_centred(qk_pre, conv_w, conv_b))
    q, k = jnp.split(u, 2, axis=-1)

    def heads(a):
        return a.reshape(b, t, MLSTM_HEADS, MLSTM_DH).transpose(0, 2, 1, 3).astype(jnp.float32)

    g = gates.astype(jnp.float32) + gate_b.reshape(-1).astype(jnp.float32)
    g = g.reshape(b, t, 4, MLSTM_HEADS).transpose(2, 0, 3, 1)
    return heads(q), heads(k) * (MLSTM_DH ** -0.5), heads(v), g

def mlstm_bidirectional(lat, ctx, need_ctx_out):
    qx, kx, vx, gx = lat
    qc, kc, vc, gc = ctx
    bq = qx.shape[0]
    zero = (jnp.zeros((bq, MLSTM_HEADS, MLSTM_DH, MLSTM_DH), jnp.float32),
            jnp.zeros((bq, MLSTM_HEADS, MLSTM_DH), jnp.float32),
            jnp.zeros((bq, MLSTM_HEADS), jnp.float32))
    hx_tot = jnp.zeros(qx.shape, jnp.float32)
    hc_tot = jnp.zeros(qc.shape, jnp.float32)
    for d in range(2):
        sx = [qx, kx, vx, gx[2 * d], jax.nn.log_sigmoid(gx[2 * d + 1])]
        sc = [qc, kc, vc, gc[2 * d], jax.nn.log_sigmoid(gc[2 * d + 1])]
        if d == 1:
            sx = [jnp.flip(a, axis=2) for a in sx]
            sc = [jnp.flip(a, axis=2) for a in sc]
        if need_ctx_out:
            hc, st = mlstm_chunkwise(sc[0], sc[1], sc[2], sc[3], sc[4], zero)
            hc_tot = hc_tot + (jnp.flip(hc, axis=2) if d == 1 else hc)
        else:
            st = mlstm_state_update(zero, sc[1], sc[2], sc[3], jnp.cumsum(sc[4], axis=-1))
        hx, _ = mlstm_chunkwise(sx[0], sx[1], sx[2], sx[3], sx[4], st)
        hx_tot = hx_tot + (jnp.flip(hx, axis=2) if d == 1 else hx)
    return hx_tot, hc_tot

def merge_groups(a, hm, o, p):
    b, t, _ = o.shape
    hm = jnp.swapaxes(hm, 1, 2) * jax.nn.sigmoid(o.astype(jnp.float32)).reshape(b, t, MLSTM_HEADS, MLSTM_DH)
    hm = head_layer_norm(hm, p['mlstm_norm']).astype(a.dtype)
    return jnp.concatenate([rms_norm(a, p['attn_out_norm']), hm], axis=-1) @ p['w_out']

def mixer(hx, hc, cos, sin, p, need_ctx_out):
    b, s, _ = hx.shape
    cq_x, ckv_x, kr_x, qk_x, v_x, o_x, g_x = split_in(hx @ p['w_in'])
    cq_c, ckv_c, kr_c, qk_c, v_c, o_c, g_c = split_in(hc @ p['w_in'])
    k_c, va_c = mla_keys(ckv_c, kr_c[:, :, None, :], p['kv_norm'], p['w_ukv'])
    k_x, va_x = mla_keys(ckv_x, apply_axial_rope(kr_x[:, :, None, :], cos, sin), p['kv_norm'], p['w_ukv'])
    q_x = mla_query(cq_x, p['q_norm'], p['w_uq'])
    q_x = jnp.concatenate([q_x[..., :NOPE_DIM], apply_axial_rope(q_x[..., NOPE_DIM:], cos, sin)], axis=-1)
    k_all = jnp.concatenate([k_c, k_x], axis=1)
    v_all = jnp.concatenate([va_c, va_x], axis=1)
    a_x = blocked_attention(q_x, k_all, v_all)
    lat = mlstm_inputs(qk_x, v_x, g_x, p['conv_w'], p['conv_b'], p['gate_b'])
    ctm = mlstm_inputs(qk_c, v_c, g_c, p['conv_w'], p['conv_b'], p['gate_b'])
    m_x, m_c = mlstm_bidirectional(lat, ctm, need_ctx_out)
    y_x = merge_groups(a_x, m_x, o_x, p)
    if not need_ctx_out:
        return y_x, None
    q_c = mla_query(cq_c, p['q_norm'], p['w_uq'])
    a_c = softmax_attend(q_c, k_c, va_c).reshape(b, hc.shape[1], ATTN_WIDTH)
    return y_x, merge_groups(a_c, m_c, o_c, p)

def sandwich_in(h, m, sub, p):
    return rms_norm(h, p['norm_pre'][sub]) * (1 + m[:, 3 * sub + 1]) + m[:, 3 * sub]

def sandwich_out(h, y, m, sub, p, weight):
    return h + weight * m[:, 3 * sub + 2] * rms_norm(y, p['norm_post'][sub])

def ffn_sub(h, m, sub, j, p):
    y = swiglu(sandwich_in(h, m, sub, p), p['w_gate'][j], p['w_up'][j], p['w_down'][j])
    return sandwich_out(h, y, m, sub, p, 0.5)

def trunk_layer(x, xc, mod_x, mod_c, cos, sin, p, need_ctx_out):
    x = ffn_sub(x, mod_x, 0, 0, p)
    xc = ffn_sub(xc, mod_c, 0, 0, p)
    y_x, y_c = mixer(sandwich_in(x, mod_x, 1, p), sandwich_in(xc, mod_c, 1, p), cos, sin, p, need_ctx_out)
    x = sandwich_out(x, y_x, mod_x, 1, p, 1.0)
    x = ffn_sub(x, mod_x, 2, 1, p)
    if need_ctx_out:
        xc = sandwich_out(xc, y_c, mod_c, 1, p, 1.0)
        xc = ffn_sub(xc, mod_c, 2, 1, p)
    return x, xc

def setup_inputs(seed: int = 0) -> dict:
    key = jax.random.key(seed)
    ks = jax.random.split(key, 26)
    f32 = jnp.float32
    L, D = DEPTH, D_MODEL

    def nrm(k, shape, fan):
        return jax.random.normal(k, shape, f32) * (fan ** -0.5)

    def gain(k, shape):
        return 1.0 + 0.05 * jax.random.normal(k, shape, f32)

    i_bias = 0.1 * jax.random.normal(ks[20], (L, 2, MLSTM_HEADS), f32)
    f_bias = jnp.linspace(3.0, 6.0, MLSTM_HEADS, dtype=f32) + 0.1 * jax.random.normal(ks[21], (L, 2, MLSTM_HEADS), f32)
    return {
        'x': jax.random.normal(ks[0], (BATCH, SEQ, D), f32),
        'c': jax.random.normal(ks[1], (BATCH, D), f32),
        'ctx': jax.random.normal(ks[2], (BATCH, CTX_LEN, D), f32),
        'c_ctx': jax.random.normal(ks[3], (D,), f32),
        'w_mod': 0.5 * nrm(ks[4], (L, D, N_MOD * D), D),
        'b_mod': 0.02 * jax.random.normal(ks[5], (L, N_MOD * D), f32),
        'norm_pre': gain(ks[6], (L, 3, D)),
        'norm_post': gain(ks[7], (L, 3, D)),
        'ffn_w_gate': nrm(ks[8], (L, 2, D, D_FF), D),
        'ffn_w_up': nrm(ks[9], (L, 2, D, D_FF), D),
        'ffn_w_down': nrm(ks[10], (L, 2, D_FF, D), D_FF),
        'w_in': nrm(ks[11], (L, D, D_IN), D),
        'q_norm': gain(ks[12], (L, Q_LORA)),
        'w_uq': nrm(ks[13], (L, Q_LORA, ATTN_HEADS * (NOPE_DIM + ROPE_DIM)), Q_LORA),
        'kv_norm': gain(ks[14], (L, KV_LORA)),
        'w_ukv': nrm(ks[15], (L, KV_LORA, ATTN_HEADS * (NOPE_DIM + V_DIM)), KV_LORA),
        'attn_out_norm': gain(ks[16], (L, ATTN_WIDTH)),
        'conv_w': nrm(ks[17], (L, CONV_K, 2 * MLSTM_WIDTH), CONV_K),
        'conv_b': 0.02 * jax.random.normal(ks[18], (L, 2 * MLSTM_WIDTH), f32),
        'gate_b': jnp.stack([i_bias, f_bias], axis=2).reshape(L, 4, MLSTM_HEADS),
        'mlstm_norm': gain(ks[19], (L, MLSTM_WIDTH)),
        'w_out': nrm(ks[22], (L, MIX_WIDTH, D), MIX_WIDTH),
    }

def reference(x, c, ctx, c_ctx, w_mod, b_mod, norm_pre, norm_post, ffn_w_gate, ffn_w_up, ffn_w_down,
              w_in, q_norm, w_uq, kv_norm, w_ukv, attn_out_norm, conv_w, conv_b, gate_b, mlstm_norm, w_out):
    bsz, n_tok, d = x.shape
    cos, sin = axial_rope_tables(n_tok)
    xc = ctx
    for l in range(DEPTH):
        p = {'norm_pre': norm_pre[l], 'norm_post': norm_post[l], 'w_gate': ffn_w_gate[l],
             'w_up': ffn_w_up[l], 'w_down': ffn_w_down[l], 'w_in': w_in[l], 'q_norm': q_norm[l],
             'w_uq': w_uq[l], 'kv_norm': kv_norm[l], 'w_ukv': w_ukv[l],
             'attn_out_norm': attn_out_norm[l], 'conv_w': conv_w[l], 'conv_b': conv_b[l],
             'gate_b': gate_b[l], 'mlstm_norm': mlstm_norm[l], 'w_out': w_out[l]}
        mod_x = (jax.nn.silu(c) @ w_mod[l] + b_mod[l]).reshape(bsz, N_MOD, 1, d)
        mod_c = (jax.nn.silu(c_ctx) @ w_mod[l] + b_mod[l]).reshape(1, N_MOD, 1, d)
        x, xc = trunk_layer(x, xc, mod_x, mod_c, cos, sin, p, l < DEPTH - 1)
    return x


_drawn_inputs = setup_inputs


def setup_inputs(seed=0):
    import zlib

    import numpy as np

    out = dict(_drawn_inputs(seed))
    spreads = {}
    factors = {'q_norm': 8.0,
     'kv_norm': 3.548,
     'attn_out_norm': 3.681,
     'conv_b': 8.0,
     'mlstm_norm': 3.385}
    for name, (base, spread) in spreads.items():
        noise = np.random.default_rng([zlib.crc32(name.encode()), seed]).standard_normal(out[name].shape)
        drawn = base * np.exp(spread * noise) if base else spread * noise
        out[name] = __import__('jax').numpy.asarray(drawn.astype(out[name].dtype))
    for name, factor in factors.items():
        out[name] = (out[name] * factor).astype(out[name].dtype)
    return out
```

```python
from contextlib import ExitStack

import numpy as np
import concourse.bass as bass
from concourse import mybir

F32 = mybir.dt.float32
F32R = mybir.dt.float32r
ALU = mybir.AluOpType
ACT = mybir.ActivationFunctionType
AX = mybir.AxisListType

P = 128
D = 1024
KD = D // P
SEQ = 512
CTX = 256
T = CTX + SEQ
NT = T // P
NTC = CTX // P
L = 2
FF = 2752
NMOD = 9
EPS = 1e-6
GRID_W = 64
HEADS = 4
QL, KVL, NOPE, ROPE, VD = 256, 128, 128, 64, 128
SM_SCALE = float((NOPE + ROPE) ** -0.5)
MH, MDH = 4, 128
K_SCALE = float(MDH ** -0.5)
MW = MH * MDH
D_IN = QL + KVL + ROPE + 4 * MW + 4 * MH
IN_CQ, IN_CKV, IN_KR = 0, QL, QL + KVL
IN_QK = IN_KR + ROPE
IN_V = IN_QK + 2 * MW
IN_O = IN_V + MW
IN_END = D_IN

NCH = -(-FF // P)
LAST_F = FF - P
OVER = NCH * P - FF
GROUPS = [(0, 8), (8, 8), (16, 6)]
GMAX = 8
RAW, CONV, MODR = 4, 2, 2
HW = 384

NBM = NMOD * KD
VA_PRE, VA_POST, VA_N = NBM, NBM + 3 * KD, NBM + 6 * KD
VB_CW, VB_CB, VB_QN, VB_KVN, VB_AN, VB_MN, VB_C, VB_CC, VB_N = 0, 24, 32, 34, 35, 39, 43, 51, 59

C_ID = 0
C_ONES = C_ID + P
C_SWQ = C_ONES + P
C_KD = C_SWQ + P
C_KSW = C_KD + P
C_SELI = C_KSW + P
C_SELF = C_SELI + 36
C_MF = C_SELF + 36
C_MB = C_MF + P
C_COS = C_MB + P
C_SIN = C_COS + T
C_N = C_SIN + T
C_PERS = C_COS
GROW = 36
GATE_AT = P - 4 * MH


def constants():
    c = np.zeros((P, C_N), np.float32)
    c[:, C_ID:C_ID + P] = np.eye(P)
    c[:, C_ONES:C_ONES + P] = 1.0 / D
    half = ROPE // 4
    for m in range(P):
        r = m % ROPE
        base = m - r
        lo = (r // half) % 2 == 0
        src = r + half if lo else r - half
        c[base + src, C_SWQ + m] = -1.0 if lo else 1.0
        c[r, C_KD + m] = 1.0
        c[src, C_KSW + m] = -1.0 if lo else 1.0
    for h in range(MH):
        c[GATE_AT + 0 * MH + h, C_SELI + h] = 1.0
        c[GATE_AT + 2 * MH + h, C_SELI + 32 + h] = 1.0
        c[GATE_AT + 1 * MH + h, C_SELF + h] = 1.0
        c[GATE_AT + 3 * MH + h, C_SELF + 32 + h] = 1.0
    s, t = np.arange(P)[:, None], np.arange(P)[None, :]
    c[:, C_MF:C_MF + P] = np.where(s <= t, 0.0, -1e30)
    c[:, C_MB:C_MB + P] = np.where(s >= t, 0.0, -1e30)
    f = np.float32
    inv = f(10000.0) ** (-np.arange(half, dtype=f) / f(half))
    pos = np.arange(SEQ)
    for m in range(P):
        axis, fr = (m % ROPE) // (2 * half), m % half
        p = (pos // GRID_W if axis == 0 else pos % GRID_W).astype(f)
        c[m, C_COS:C_COS + CTX] = 1.0
        c[m, C_COS + CTX:C_COS + T] = np.cos(p * inv[fr])
        c[m, C_SIN + CTX:C_SIN + T] = np.sin(p * inv[fr])
    return c


def full_halves(l):
    return [(0, HW), (HW, HW)]


def out_halves(l):
    return [(0, HW), (HW, HW)] if l < L - 1 else [(CTX, SEQ // 2), (CTX + SEQ // 2, SEQ // 2)]


def halves_of(l, sub, post):
    return full_halves(l) if (sub, post) in ((0, 0), (0, 1), (1, 0)) else out_halves(l)


def segments(start, width):
    out = []
    if start < CTX:
        out.append((start, min(width, CTX - start), 1))
    if start + width > CTX:
        a = max(start, CTX)
        out.append((a, start + width - a, 0))
    return out


FFN_TILES = 2 * NCH + len(GROUPS) * KD
MIX_TILES = 32
def ffn_tile0(l, j): return l * (2 * FFN_TILES + MIX_TILES) + j * (FFN_TILES + MIX_TILES)
def mix_tile0(l): return l * (2 * FFN_TILES + MIX_TILES) + FFN_TILES
ALL_TILES = L * (2 * FFN_TILES + MIX_TILES)
WOUT_TILE = 24
def tile_units(t):
    for l in range(L):
        i = t - mix_tile0(l)
        if 0 <= i < MIX_TILES:
            if 4 <= i < 8 or 16 <= i < 20:
                return 1 if i not in (7, 19) else (NT if i == 7 else len(o_tts(l)))
            return {20: 2 * HEADS, 21: NT, 22: 2 * HEADS, 23: 4}.get(i, 2)
    return 2
def units_before(t): return sum(tile_units(i) for i in range(t))
def unit_of(l, i, n):
    return units_before(mix_tile0(l) + i) + n + 1
def feat_unit(l, f, n):
    if f < 12:
        return unit_of(l, f if f < 4 else f + 4, n)
    i, f0 = (20, 12) if f < 16 else (22, 16) if f < 20 else (23, 20)
    return unit_of(l, i, 2 * (f - f0) + n)
def ffn_pair0(l, j): return 2 * NCH * (2 * l + j)
DOWN_FFN = 2 * KD * len(GROUPS)
DOWN_OUT = 2 * KD
def ffn_down0(l, j): return l * (2 * DOWN_FFN + DOWN_OUT) + j * (DOWN_FFN + DOWN_OUT)
def out_down0(l): return l * (2 * DOWN_FFN + DOWN_OUT) + DOWN_FFN
def stat_event(l, sub, post, n): return 12 * l + 4 * sub + 2 * post + n
def pre_event(l, sub, n): return 6 * l + 2 * sub + n
def post_event(l, sub, n): return 6 * l + 2 * sub + n
MOD_UNITS = 2 * NMOD
FIRST_UNITS = 6
def mod_unit0(l, j, g):
    if j == 0 and g < 2:
        return l * MOD_UNITS + FIRST_UNITS + 6 * g
    if j == 1 and l + 1 < L and g == 0:
        return (l + 1) * MOD_UNITS
    return None

N_FEAT = 22
def attn_items(l):
    lat = [(h, tt) for h in range(HEADS) for tt in range(NTC, NT)]
    return ([(h, tt) for h in range(HEADS) for tt in range(NTC)] if l < L - 1 else []) + lat
def items_before(l): return 0 if l == 0 else len(attn_items(0))
def o_tts(l): return list(range(NT)) if l < L - 1 else list(range(NTC, NT))
def triples(l): return [[0, 1, 2], [3, 4, 5]] if l < L - 1 else [[2, 3], [4, 5]]
OUT_UNITS = MH * 2 * 2


def source_blocks(l, d, j):
    lat = (CTX, SEQ)
    if j < NTC:
        if l == L - 1:
            return None, [lat]
        rest = (P * (j + 1), CTX - P * (j + 1)) if d == 0 else (0, P * j)
        return j, [r for r in (rest, lat) if r[1]]
    rest = (P * (j + 1), T - P * (j + 1)) if d == 0 else (CTX, P * j - CTX)
    return j, [r for r in (rest,) if r[1]]


def sources_of(d, tt):
    if tt < NTC:
        return list(range(0, tt + 1)) if d == 0 else list(range(tt, NTC))
    return list(range(NTC)) + (list(range(NTC, tt + 1)) if d == 0 else list(range(tt, NT)))


def source_slots(l, d):
    out = {}
    for j in range(NT):
        for tt in range(NTC if l == L - 1 else 0, NT):
            if j in sources_of(d, tt):
                out[j, tt] = len(out)
    return out


def product_ranges(l, d, j):
    slots = source_slots(l, d)
    out = []
    for part in (range(NTC), range(NTC, NT)):
        tts = [tt for tt in part if (j, tt) in slots]
        if tts:
            out.append((slots[j, tts[0]], tts[0] * P, len(tts) * P))
    return out


BLOCKS = 2 * NT * MH
def block_index(l, h, j, d): return BLOCKS * l + 2 * NT * h + 2 * j + d
def diag_index(l, h, j, d):
    if l == 0:
        return 2 * NT * h + 2 * j + d
    return BLOCKS + 2 * (NT - NTC) * h + 2 * (j - NTC) + d
def turned_by_dve(l, i):
    return (16 if l else 0) + sum(tt >= NTC for _, tt in attn_items(l)[:i + 1])
def fin_before(l): return 0 if l == 0 else NT * (1 + MH)
def o_before(l): return NT if l else 0


def hybrid_backbone_kernel(nc, x, c, ctx_in, c_ctx, w_mod, b_mod, norm_pre, norm_post, ffn_w_gate, ffn_w_up,
                           ffn_w_down, w_in, q_norm, w_uq, kv_norm, w_ukv, attn_out_norm, conv_w, conv_b, gate_b,
                           mlstm_norm, w_out, consts, out):
    stack = ExitStack()
    with stack:
        def sb(name, shape, dt=F32, on=stack):
            return on.enter_context(nc.sbuf_tensor(name, shape, dt))

        def overlay(name, shape, dt=F32):
            with nc.sbuf_tensor(name, shape, dt) as t:
                return t

        def sem(name):
            return stack.enter_context(nc.semaphore(name))

        ps = stack.enter_context(nc.psum_tensor("ps", [P, 8, 512], F32))

        xT = sb("xT", [P, KD, T])
        raw = sb("raw", [P, RAW, KD * P])
        wsp = sb("wsp", [P, CONV, 2, KD * P], F32R)
        cst = sb("cst", [P, C_PERS])
        scr = sb("scr", [P, 6, HW])
        modT = sb("modT", [P, NBM, 2])
        modN = sb("modN", [P, NBM, 2])
        vecA = sb("vecA", [P, L, VA_N])
        vecB = sb("vecB", [P, L, VB_N])
        silc = sb("silc", [P, 2, KD])
        gcol = sb("gcol", [P, 3, KD, 2])
        colt = sb("colt", [P, KD, 2])
        kc = sb("kc", [P, 4])
        epsc, onec, zeroc = kc[:, 0:1], kc[:, 1:2], kc[:, 2:3]
        sqa, sqb, tmp3, rstd = scr[:, 0], scr[:, 1], [scr[:, 2], scr[:, 3], scr[:, 4]], scr[:, 5]
        sq2 = [sqa, sqb]
        sg2, af2 = [scr[:, 0], scr[:, 1]], [scr[:, 2], scr[:, 3]]
        cv = [scr[:, 2 * n:2 * n + 2].rearrange("p a b -> p (a b)") for n in range(2)]
        rstd2 = [scr[:, 2 * n:2 * n + 2].rearrange("p a b -> p (a b)") for n in (1, 2)]
        tmpq = scr[:, 4]
        sqw = cv[0][:, 0:HEADS * VD]
        modL = [modT, modN]
        ident = cst[:, C_ID:C_ID + P]
        ones = cst[:, C_ONES:C_ONES + P]

        with ExitStack() as s:
            hnF = sb("hnF", [P, 2, KD, T], F32R, s)
            vstage = overlay("vstage", [P, 4, P])
            aT = sb("aT", [P, 2, GMAX, T], F32R, s)
            xstage = overlay("xstage", [P, NT, D])
            ostage = overlay("ostage", [P, 2, D])
            yF = sb("yF", [P, KD, T], F32, s)
            modw = sb("modw", [P, MODR, 2, 512], F32, s)
            macc = sb("macc", [P, 2, 512], F32, s)
        with ExitStack() as s:
            yM = overlay("yM", [P, KD, T])
            qkT = sb("qkT", [P, KD, T], F32, s)
            rows = overlay("rows", [P, 4, T])
            otok = sb("otok", [P, NT, MW], F32, s)
            vext = sb("vext", [P, NT, MH, MDH + 1], F32, s)
            negG = sb("negG", [P, T], F32, s)
            krT = sb("krT", [P, T], F32, s)
            gb = sb("gb", [P, 2], F32, s)
            colF = sb("colF", [P, NT, GROW], F32, s)
            expnm = sb("expnm", [P, NT, GROW], F32, s)
            stat = sb("stat", [P, 4, 32], F32, s)
            bn6 = sb("bn6", [P, 2, 6], F32, s)
            mv = sb("mv", [P, MH * NT, 2], F32, s)
            cqn = overlay("cqn", [P, 2, 2, T], F32R)
            atok = sb("atok", [P, NT, HEADS * VD], F32, s)
            ckn = sb("ckn", [P, 2, T], F32R, s)
            mixT = overlay("mixT", [P, 2, KD, T], F32R)
            with ExitStack() as w:
                hnM = sb("hnM", [P, 2, KD, T], F32R, w)
                cosT = sb("cosT", [P, 2, T], F32, w)
                krt = sb("krt", [P, 2, HW], F32, w)
            with ExitStack() as w:
                qnT = sb("qnT", [P, HEADS, T], F32, w)
                knT = sb("knT", [P, HEADS, T], F32, w)
                va = sb("va", [P, NT, HEADS * VD], F32, w)
                qrT = sb("qrT", [P, 2, T], F32, w)
                pbuf = sb("pbuf", [P, 2, T], F32, w)
                sb("cosT_stays", [P, 2, T], F32, w)
                ptb = sb("ptb", [P, 2, NT, P], F32, w)
            with ExitStack() as w:
                pblk = sb("pblk", [P, 2, 2, 21, P], F32, w)
                gbc = sb("gbc", [P, 2, T], F32, w)
                dbuf = sb("dbuf", [P, 2, T], F32, w)
                hh = sb("hh", [P, NT, MDH], F32, w)
                ht = sb("ht", [P, 3, MDH], F32, w)
                dn = sb("dn", [P, 2, 4], F32, w)
        krg, ckv, cq = qkT[:, 7], qkT[:, 6], qkT[:, 4:6]
        rI, rX, rT, rB = (rows[0:GROW, n] for n in range(4))

        cst_in, vec_in, x_in, tab_in, gb_in = (sem(n) for n in ("cst_in", "vec_in", "x_in", "tab_in", "gb_in"))
        raw_in = [sem(f"raw_in{n}") for n in range(RAW)]
        mod_in = [sem(f"mod_in{n}") for n in range(MODR)]
        whi_done, wlo_done, unit_done = sem("whi_done"), sem("wlo_done"), sem("unit_done")
        silu_done, amul_done, ahi_done, alo_done, yadd_done = (
            sem(n) for n in ("silu_done", "amul_done", "ahi_done", "alo_done", "yadd_done"))
        mod_step, mod_tr, mod_sum = sem("mod_step"), sem("mod_tr"), sem("mod_sum")
        sq_done, stat_mm, std_done, rstd_done = (sem(n) for n in ("sq_done", "stat_mm", "std_done", "rstd_done"))
        xr_done, hn_done, hhi_done, hlo_done, yr_done, x_done = (
            sem(n) for n in ("xr_done", "hn_done", "hhi_done", "hlo_done", "yr_done", "x_done"))
        xtr, xev = sem("xtr"), sem("xev")
        vtr, vev = sem("vtr"), sem("vev")
        otr, oev, o_out = sem("otr"), sem("oev"), [sem("o_out0"), sem("o_out1")]
        dchain, achain = sem("dchain"), sem("achain")
        ones_done, gbz_done, pad_done = sem("ones_done"), sem("gbz_done"), sem("pad_done")
        feat_out = sem("feat_out")
        v_out, o_outs, va_out = sem("v_out"), sem("o_outs"), sem("va_out")
        sel_done, gates_out, kro_out = sem("sel_done"), sem("gates_out"), sem("kro_out")
        lsq_done, lstat_done, lstd_done, lat_done = (sem(n) for n in ("lsq_done", "lstat_done", "lstd_done", "lat_done"))
        nabs_done, lnf_done, rows_done, rtr_done, colF_done, expnm_done = (
            sem(n) for n in ("nabs_done", "lnf_done", "rows_done", "rtr_done", "colF_done", "expnm_done"))
        cmid_done, ctap_done, conv_done = sem("cmid_done"), sem("ctap_done"), sem("conv_done")
        sw_done, qr_out = sem("sw_done"), sem("qr_out")
        sc_done, max_done, exp_done, pt_done, pta_out, ptd_out, pv_done, pv_out = (
            sem(n) for n in ("sc_done", "max_done", "exp_done", "pt_done", "pta_out", "ptd_out", "pv_done", "pv_out"))
        g_done, g_out, s_done, dg_done, dx_done, pb_done, mo_done, mo_out = (
            sem(n) for n in ("g_done", "g_out", "s_done", "dg_done", "dx_done", "pb_done", "mo_done", "mo_out"))
        fvar_done, fstd_done, fin_done = sem("fvar_done"), sem("fstd_done"), sem("fin_done")
        mt_done, mhi_done, mlo_done = sem("mt_done"), sem("mhi_done"), sem("mlo_done")

        block = stack.enter_context(nc.Block())

        def hn_of(sub):
            return hnM if sub == 1 else hnF

        def y_of(sub):
            return yM if sub == 1 else yF

        @block.sync
        def _(sp):
            def load_tile(t, slot, parts):
                sp.wait_ge(wlo_done, t - RAW + 1 + RAW)
                for dst, src in parts:
                    sp.dma_start(dst, src).then_inc(raw_in[slot], 16)

            def load_mod(u, lm, ul, which):
                w = w_mod[lm].rearrange("(k p) n -> p k n", p=P)
                for j in range(4)[which]:
                    m = 4 * u + j
                    sp.wait_ge(mod_step, 4 * (m - MODR + 1))
                    sp.dma_start(modw[:, j % MODR], w[:, 2 * j:2 * j + 2, bass.ds(512 * ul, 512)]).then_inc(
                        mod_in[j % MODR], 16)

            def cols_tile(slot, w, at, width=P, k=KD):
                dst = raw[:, slot].rearrange("p (k f) -> p k f", f=P)
                src = w.rearrange("(k p) f -> p k f", p=P)
                h = k // 2
                return [(dst[:, a:b], src[:, a:b, at]) for a, b in ((0, h), (h, k))]

            def ffn(l, j):
                t0 = ffn_tile0(l, j)
                wg, wu, wd = ffn_w_gate[l, j], ffn_w_up[l, j], ffn_w_down[l, j]
                for g, (c0, G) in enumerate(GROUPS):
                    u0 = mod_unit0(l, j, g)

                    def up_body(i, cols):
                        t = t0 + 4 * i
                        for b in range(2):
                            for wi, w in enumerate((wg, wu)):
                                s = 2 * b + wi
                                load_tile(t + s, s, cols_tile(s, w, cols[b]))
                                if u0 is not None:
                                    load_mod(u0 + i, u0 // MOD_UNITS, u0 % MOD_UNITS + i, slice(s, s + 1))

                    if u0 is not None and j == 1:
                        sp.wait_ge(unit_done, units_before(ffn_tile0(l, j)))
                    n = G // 2 - (g == len(GROUPS) - 1)
                    with sp.Fori(0, n) as i:
                        up_body(i, [bass.ds((c0 + 2 * i + b) * P, P) for b in range(2)])
                    if n < G // 2:
                        up_body(n, [slice((NCH - 2) * P, (NCH - 1) * P), slice(LAST_F, FF)])
                    t0 += 2 * G
                    if u0 is not None:
                        u0 += G // 2

                    def down_body(i):
                        for s in range(4):
                            cols = bass.ds((4 * i + s) * P, P)
                            if G == GMAX:
                                parts = cols_tile(s, wd[c0 * P:(c0 + G) * P], cols, k=G)
                            else:
                                parts = [(raw[:, s, 0:(G - 1) * P].rearrange("p (k f) -> p k f", f=P),
                                          wd[c0 * P:(c0 + G - 1) * P].rearrange("(k p) f -> p k f", p=P)[:, :, cols]),
                                         (raw[:, s, (G - 1) * P:G * P], wd[LAST_F:FF, cols])]
                            load_tile(t0 + 4 * i + s, s, parts)
                            if u0 is not None:
                                load_mod(u0 + i, u0 // MOD_UNITS, u0 % MOD_UNITS + i, slice(s, s + 1))

                    with sp.Fori(0, KD // 4) as i:
                        down_body(i)
                    t0 += KD

            def mixer(l):
                t = mix_tile0(l)
                w = w_in[l]

                def put(parts):
                    nonlocal t
                    load_tile(t, t % RAW, parts)
                    t += 1

                if l > 0:
                    sp.wait_ge(expnm_done, l)
                sp.wait_ge(gbz_done, l + 1)
                for n, (r, g) in enumerate(((0, 0), (32, 2), (0, 1), (32, 3))):
                    sp.dma_start(gb[r:r + MH, n // 2:n // 2 + 1], gate_b[l, g].rearrange("(h o) -> h o", o=1)
                                 ).then_inc(gb_in, 16)
                sp.wait_ge(unit_done, units_before(mix_tile0(l)))
                sp.dma_start(cosT[:], consts[:, C_COS:C_COS + 2 * T].rearrange("p (a t) -> p a t", a=2)
                             ).then_inc(tab_in, 16)
                dst = raw[:, t % RAW].rearrange("p (k f) -> p k f", f=P)
                src = w.rearrange("(k p) f -> p k f", p=P)
                put([(dst[:, :, 0:ROPE], src[:, :, IN_KR:IN_KR + ROPE]),
                     (dst[:, :, ROPE:P], src[:, :, IN_END - (P - ROPE):IN_END])])
                for a in (IN_CKV, IN_CQ, IN_CQ + P):
                    put(cols_tile(t % RAW, w, slice(a, a + P)))

                def token_major(a):
                    for q in range(4):
                        dst = raw[:, t % RAW].rearrange("p (k f) -> p k f", f=MW)
                        put([(dst[:, k], w[(2 * q + k) * P:(2 * q + k + 1) * P, a:a + MW]) for k in range(2)])

                token_major(IN_V)
                for n in range(KD):
                    put(cols_tile(t % RAW, w, slice(IN_QK + n * P, IN_QK + (n + 1) * P)))
                token_major(IN_O)
                kv = w_ukv[l].rearrange("p (h c) -> p h c", c=NOPE + VD)
                for a in (0, NOPE):
                    dst = raw[:, t % RAW, 0:HEADS * P].rearrange("p (h f) -> p h f", f=P)
                    put([(dst[:, 2 * b:2 * b + 2], kv[:, 2 * b:2 * b + 2, a:a + P]) for b in range(2)])
                uq = w_uq[l].rearrange("(k p) (h c) -> p k h c", p=P, c=NOPE + ROPE)
                dst = raw[:, t % RAW].rearrange("p (k h f) -> p k h f", k=2, f=NOPE)
                put([(dst[:, k], uq[:, k, :, 0:NOPE]) for k in range(2)])
                dst = raw[:, t % RAW, 0:2 * HEADS * ROPE].rearrange("p (k h f) -> p k h f", k=2, f=ROPE)
                put([(dst[:, k], uq[:, k, :, NOPE:NOPE + ROPE]) for k in range(2)])
                for n in range(KD):
                    put(cols_tile(t % RAW, w_out[l], slice(n * P, (n + 1) * P)))
                assert t == mix_tile0(l) + MIX_TILES

            sp.dma_start(cst[:], consts[:, 0:C_PERS]).then_inc(cst_in, 16)
            for l in range(L):
                for dst, at, v in (
                    (vstage[:, 2 * l], 0, b_mod[l].rearrange("(r f) -> r f", f=P)),
                    (vstage[:, 2 * l], VA_PRE, norm_pre[l].rearrange("s (r f) -> (s r) f", f=P)),
                    (vstage[:, 2 * l], VA_POST, norm_post[l].rearrange("s (r f) -> (s r) f", f=P)),
                    (vstage[:, 2 * l + 1], VB_CW, conv_w[l].rearrange("s (r f) -> (s r) f", f=P)),
                    (vstage[:, 2 * l + 1], VB_CB, conv_b[l].rearrange("(r f) -> r f", f=P)),
                    (vstage[:, 2 * l + 1], VB_QN, q_norm[l].rearrange("(r f) -> r f", f=P)),
                    (vstage[:, 2 * l + 1], VB_KVN, kv_norm[l].rearrange("(r f) -> r f", f=P)),
                    (vstage[:, 2 * l + 1], VB_AN, attn_out_norm[l].rearrange("(r f) -> r f", f=P)),
                    (vstage[:, 2 * l + 1], VB_MN, mlstm_norm[l].rearrange("(r f) -> r f", f=P)),
                    (vstage[:, 2 * l + 1], VB_C, c.rearrange("b (r f) -> (b r) f", f=P)),
                    (vstage[:, 2 * l + 1], VB_CC, c_ctx.rearrange("(r f) -> r f", f=P)),
                ):
                    sp.dma_start(dst[at:at + v.shape[0]], v).then_inc(vec_in, 16)
            sp.dma_start(xstage[:, 0:NTC], ctx_in[0].rearrange("(t p) d -> p t d", p=P)).then_inc(x_in, 16)
            sp.dma_start(xstage[:, NTC:NT], x[0].rearrange("(t p) d -> p t d", p=P)).then_inc(x_in, 16)
            w = w_mod[0].rearrange("(k p) n -> p k n", p=P)
            for m in range(MODR):
                sp.dma_start(modw[:, m], w[:, 2 * m:2 * m + 2, 0:512]).then_inc(mod_in[m], 16)
            load_mod(0, 0, 0, slice(MODR, 4))
            with sp.Fori(1, FIRST_UNITS) as i:
                load_mod(i, 0, i, slice(0, 4))
            for l in range(L):
                ffn(l, 0)
                mixer(l)
                ffn(l, 1)
            for n in range(SEQ // P):
                sp.wait_ge(oev, 2 * (n + 1))
                sp.dma_start(out[0, n * P:(n + 1) * P, :], ostage[:, n % 2]).then_inc(o_out[n % 2], 16)
            for n in range(2):
                sp.wait_ge(o_out[n], 16 * (SEQ // P // 2))

        @block.gpsimd
        def _(pool):
            for l in range(L):
                pool.wait_ge(unit_done, units_before(mix_tile0(l)))
                pool.wait_ge(alo_done, ffn_pair0(l, 0) + 2 * NCH + 2)
                pool.memset(gb[:], 0.0).then_inc(gbz_done, 1)
                pool.memset(vext[:, :, :, MDH:MDH + 1], 1.0).then_inc(ones_done, 1)

        @block.scalar
        def _(act):
            chain = [0]

            def link(ins):
                chain[0] += 1
                ins.then_inc(achain, 1)
                act.wait_ge(achain, chain[0])

            def w_hi(t, slot, cs, nth, used):
                act.wait_ge(raw_in[slot], 32 * nth)
                if used is not None:
                    act.wait_ge(unit_done, used)
                act.activation(wsp[:, cs, 0], raw[:, slot], ACT.Copy).then_inc(whi_done, 1)

            def squares(l, sub, post, n, src, ready):
                a, w = halves_of(l, sub, post)[n]
                e = stat_event(l, sub, post, n)
                for k in range(KD):
                    ready(k)
                    i = KD * e + k
                    if i >= 2:
                        act.wait_ge(stat_mm, i - 1)
                    act.activation(sq2[k % 2][:, 0:w], src[:, k, a:a + w], ACT.Square).then_inc(sq_done, 1)
                act.wait_ge(stat_mm, KD * (e + 1))
                bank = ps[:, 6 + n, 0:w]
                act.activation(bank, bank, ACT.Sqrt, bias=epsc).then_inc(std_done, 1)

            def pre(l, sub, n):
                a, w = halves_of(l, sub, 0)[n]

                def ready(k):
                    if l == 0 and sub == 0:
                        act.wait_ge(xev, 2 * KD)
                    else:
                        act.wait_ge(x_done, KD * (post_event(l, sub, n) - 2) + k + 1)
                squares(l, sub, 0, n, xT, ready)
                hn = hn_of(sub)
                p = pre_event(l, sub, n)
                for k in range(KD):
                    act.wait_ge(hn_done, KD * p + k + 1)
                    act.activation(hn[:, 0, k, a:a + w], tmp3[k % 3][:, 0:w], ACT.Copy).then_inc(hhi_done, 1)

            def ffn(l, j):
                t0, q0 = ffn_tile0(l, j), ffn_pair0(l, j)
                hv = halves_of(l, 2 * j, 1)
                for g, (c0, G) in enumerate(GROUPS):
                    def up_body(i, last):
                        for b in range(2):
                            t = t0 + 4 * i + 2 * b
                            q = q0 + 4 * i + 2 * b
                            used = units_before(t0) + 8 * i + 4 * b
                            s = 2 * b
                            for n, (a, w) in enumerate(hv):
                                act.wait_ge(unit_done, used + n + 1)
                                act.activation(sg2[n][:, 0:w], ps[:, n, 0:w], ACT.Silu).then_inc(silu_done, 1)
                            w_hi(t + 2, (s + 2) % RAW, 0, (t0 + 2 * b + 2) // RAW + 1 + i, used + 2)
                            kc = 2 * i + b
                            for n, (a, w) in enumerate(hv):
                                act.wait_ge(amul_done, q + n + 3)
                                lo = OVER if last and b == 1 else 0
                                act.activation(aT[lo:P, 0, kc, a:a + w], af2[n][lo:P, 0:w], ACT.Copy
                                               ).then_inc(ahi_done, 1)
                            w_hi(t + 3, (s + 3) % RAW, 1, (t0 + 2 * b + 3) // RAW + 1 + i, used + 4)

                    n_loop = G // 2 - (g == len(GROUPS) - 1)
                    with act.Fori(0, n_loop) as i:
                        up_body(i, False)
                    if n_loop < G // 2:
                        up_body(n_loop, True)
                    t0 += 2 * G
                    q0 += 2 * G

                    def down_body(i):
                        for s in range(4):
                            t = t0 + 4 * i + s
                            if isinstance(t, int) and t + CONV >= ALL_TILES:
                                continue
                            w_hi(t + 2, (s + 2) % RAW, s % 2, (t0 + s + 2) // RAW + 1 + i,
                                 units_before(t0) + 8 * i + 2 * s + 2)

                    if l == L - 1 and j == 1 and g == len(GROUPS) - 1:
                        for i in range(KD // 4):
                            down_body(i)
                    else:
                        with act.Fori(0, KD // 4) as i:
                            down_body(i)
                    t0 += KD

            def post_sq(l, sub, n):
                d0 = (out_down0(l) if sub == 1 else ffn_down0(l, sub // 2) + DOWN_FFN - DOWN_OUT)
                squares(l, sub, 1, n, y_of(sub), lambda k: act.wait_ge(yadd_done, d0 + 2 * k + n + 3))

            def mixer(l):
                t0 = mix_tile0(l)
                fb = 2 * N_FEAT * l

                def hi_after(i):
                    t = t0 + i
                    w_hi(t + 2, (t + 2) % RAW, t % 2, (t + 2) // RAW + 1, units_before(t + 1))

                def evac(f, dst, halves):
                    for n, (a, w) in enumerate(halves):
                        act.wait_ge(unit_done, feat_unit(l, f, n))
                        act.activation(dst[:, a:a + w], ps[:, 2 * (f % 2) + n, 0:w], ACT.Copy).then_inc(feat_out, 1)

                fh, oh = full_halves(l), out_halves(l)
                act.wait_ge(unit_done, units_before(t0))
                evac(0, krg, fh)
                hi_after(0)
                evac(1, ckv, fh)
                hi_after(1)
                act.wait_ge(gb_in, 64 * (l + 1))
                for z, dst in enumerate((rI, rX)):
                    for n, (a, w) in enumerate(fh):
                        act.wait_ge(sel_done, 8 * l + 2 * z + n + 1)
                        act.activation(dst[:, a:a + w], ps[0:GROW, 6 + n, 0:w], ACT.Identity,
                                       bias=gb[0:GROW, z:z + 1]).then_inc(gates_out, 1)
                    evac(2 + z, cq[:, z], oh)
                    hi_after(2 + z)
                for i, (src, halves) in enumerate(((ckv, fh), (cq[:, 0], oh), (cq[:, 1], oh))):
                    for n, (a, w) in enumerate(halves):
                        if i == 2:
                            act.wait_ge(lstat_done, 6 * l + 3 + n)
                        if i == 1:
                            act.wait_ge(lstat_done, 6 * l + 1 + n)
                        act.wait_ge(feat_out, fb + 2 * (i + 1) + n + 1)
                        act.activation(sq2[n][:, 0:w], src[:, a:a + w], ACT.Square).then_inc(lsq_done, 1)
                    if i != 1:
                        for n, (a, w) in enumerate(halves):
                            act.wait_ge(lstat_done, 6 * l + 2 * i + n + 1)
                            act.activation(rstd2[i // 2][:, a:a + w], ps[:, 6 + n, 0:w], ACT.Sqrt, bias=epsc,
                                           scale=float(D // (KVL if i == 0 else QL))).then_inc(lstd_done, 1)
                hi_after(4)
                act.wait_ge(nabs_done, l + 1)
                link(act.activation(rT, rT, ACT.Exp))
                act.activation(rT, rT, ACT.Ln, bias=onec[0:GROW]).then_inc(lnf_done, 1)
                for i in range(5, 8):
                    hi_after(i)
                for n in range(KD):
                    f = 4 + n
                    halves = oh if n < MH else fh
                    if n == 1:
                        act.wait_ge(lat_done, 6 * (l + 1))
                    u = qkT[:, n]
                    evac(f, u, halves)
                    hi_after(8 + n)
                    act.wait_ge(feat_out, fb + 2 * f + 2)
                    lo = halves[0][0]
                    act.activation(cv[n % 2][:, lo:T], u[:, lo:T], ACT.Identity, bias=vecB[:, l, VB_CB + n:VB_CB + n + 1],
                                   scale=vecB[:, l, VB_CW + KD + n:VB_CW + KD + n + 1]).then_inc(cmid_done, 1)
                    if n >= 1:
                        silu_conv(l, n - 1)
                silu_conv(l, KD - 1)
                act.wait_ge(rtr_done, 2 * (l + 1))
                act.activation(expnm[:].rearrange("p a b -> p (a b)"), ps[:, 7, 0:NT * GROW], ACT.Exp
                               ).then_inc(expnm_done, 1)
                for i in range(16, 20):
                    hi_after(i)
                for i, tt in enumerate(o_tts(l)):
                    act.wait_ge(unit_done, unit_of(l, 19, i))
                    if i == 0:
                        act.wait_ge(colF_done, l + 1)
                    act.activation(otok[:, tt], ps[:, tt], ACT.Sigmoid).then_inc(o_outs, 1)
                for h in range(HEADS):
                    evac(12 + h, knT[:, h], fh)
                hi_after(20)
                for tt in range(NT):
                    act.wait_ge(unit_done, unit_of(l, 21, tt))
                    act.activation(va[:, tt], ps[:, tt], ACT.Copy).then_inc(va_out, 1)
                hi_after(21)
                for h in range(HEADS):
                    evac(16 + h, qnT[:, h], oh)
                hi_after(22)
                for z in range(2):
                    evac(20 + z, cv[z], oh)
                hi_after(23)
                items = attn_items(l)
                a0 = items_before(l)

                def attn_exp(i):
                    h, tt = items[i]
                    nk = T if tt >= NTC else CTX
                    act.wait_ge(max_done, a0 + i + 1)
                    if i >= 2:
                        act.wait_ge(pt_done, a0 + i - 1)
                    b = 2 * (i % 2)
                    src = ps[:, b:b + 2, 0:HW] if nk == T else ps[:, b, 0:CTX]
                    dst = pbuf[:, i % 2, 0:nk]
                    if nk == T:
                        dst = dst.rearrange("p (a b) -> p a b", a=2)
                    act.activation(dst, src, ACT.Exp, bias=stat[:, 0, i % 8:i % 8 + 1], scale=SM_SCALE,
                                   accum_out=stat[:, 1, i % 8:i % 8 + 1]).then_inc(exp_done, 1)

                def pt_evac(i):
                    h, tt = items[i]
                    act.wait_ge(pt_done, a0 + i + 1)
                    if i >= 2:
                        act.wait_ge(pv_done, a0 + i - 1)
                    ns = 4 if tt >= NTC else NTC
                    act.activation(ptb[:, i % 2, 0:ns].rearrange("p a b -> p (a b)"), ps[:, 4, 0:ns * P], ACT.Copy
                                   ).then_inc(pta_out, 1)

                for i in range(len(items) + 1):
                    if i < len(items):
                        attn_exp(i)
                    if i >= 1:
                        pt_evac(i - 1)
                for h in range(MH):
                    for d in range(2):
                        for z, (a, w) in enumerate(((0, CTX), (CTX, SEQ))):
                            gi = 4 * (MH * l + h) + 2 * d + z
                            act.wait_ge(g_done, gi + 1)
                            if h > 0:
                                act.wait_ge(dg_done, diag_index(l, h - 1, NT - 1, 1) + 1)
                            act.activation(gbc[:, d, a:a + w], ps[:, z, 0:w], ACT.Copy).then_inc(g_out, 1)
                    for j in range(NT):
                        for d in range(2):
                            diag, rest = source_blocks(l, d, j)
                            col = colF[:, j, 32 * d + h:32 * d + h + 1]
                            i = block_index(l, h, j, d)
                            if i >= 2:
                                act.wait_ge(pb_done, i - 1)
                            act.wait_ge(g_out, 4 * (MH * l + h) + 2 * d + 2)
                            ins = None
                            for a, w in rest:
                                ins = act.activation(dbuf[:, d, a:a + w], gbc[:, d, a:a + w], ACT.Exp, bias=col)
                            if diag is not None:
                                act.wait_ge(dg_done, diag_index(l, h, j, d) + 1)
                                ins = act.activation(dbuf[:, d, diag * P:(diag + 1) * P],
                                                     dbuf[:, d, diag * P:(diag + 1) * P], ACT.Exp)
                            ins.then_inc(dx_done, 1)
                act.wait_ge(fvar_done, l + 1)
                t1 = o_tts(l)[0]
                var = stat[:, 2, 0:NT * MH].rearrange("p (h t) -> p h t", h=MH)[:, :, t1:NT]
                act.activation(var, var, ACT.Sqrt, bias=epsc).then_inc(fstd_done, 1)
                act.activation(stat[:, 3, t1:NT], stat[:, 3, t1:NT], ACT.Sqrt, bias=epsc,
                               scale=1.0 / (HEADS * VD)).then_inc(fstd_done, 1)
                for cidx in range(KD):
                    for n, (a, w) in enumerate(oh):
                        i = 16 * l + 2 * cidx + n
                        act.wait_ge(mt_done, i + 1)
                        act.activation(mixT[:, 0, cidx, a:a + w], ps[:, (2 * cidx + n) % 4, 0:w], ACT.Identity,
                                       scale=vecB[:, l, VB_AN + cidx:VB_AN + cidx + 1], bias=zeroc).then_inc(mhi_done, 1)
                for i in range(KD):
                    hi_after(24 + i)

            def silu_conv(l, n):
                lo = (out_halves(l) if n < MH else full_halves(l))[0][0]
                act.wait_ge(ctap_done, KD * l + n + 1)
                act.activation(qkT[:, n, lo:T], cv[n % 2][:, lo:T], ACT.Silu).then_inc(conv_done, 1)

            act.wait_ge(vev, 4)
            act.activation(silc[:, 0], vecB[:, 0, VB_C:VB_C + KD], ACT.Silu).then_inc(silu_done, 1)
            act.activation(silc[:, 1], vecB[:, 0, VB_CC:VB_CC + KD], ACT.Silu).then_inc(silu_done, 1)
            for t in range(CONV):
                w_hi(t, t, t, 1, None)
            for l in range(L):
                for sub in range(3):
                    for n in range(2):
                        pre(l, sub, n)
                    if sub == 1:
                        mixer(l)
                    else:
                        ffn(l, sub // 2)
                    for n in range(2):
                        post_sq(l, sub, n)

        @block.vector
        def _(dve):
            chain = [0]

            def link(ins):
                chain[0] += 1
                ins.then_inc(dchain, 1)
                dve.wait_ge(dchain, chain[0])

            def w_lo(t, slot, cs):
                dve.wait_ge(whi_done, t + 1)
                dve.tensor_tensor(wsp[:, cs, 1], raw[:, slot], wsp[:, cs, 0].bitcast(F32), ALU.subtract
                                  ).then_inc(wlo_done, 1)

            def mod_tiles(u, js):
                for j in js:
                    m = 4 * u + j
                    nth = 2 * u + j // 2 + 1
                    dve.wait_ge(mod_in[j % MODR], 16 * nth)
                    for kk in range(2):
                        k = 2 * j + kk
                        w = modw[:, j % MODR, kk]
                        for v in range(2):
                            s = 16 * u + 2 * k + v
                            if k == 0:
                                if not (isinstance(u, int) and u == 0):
                                    dve.wait_ge(mod_tr, u)
                                ins = dve.tensor_scalar(macc[:, v], w, silc[:, v, k:k + 1], None, ALU.mult)
                            else:
                                dve.wait_ge(mod_step, s - 1)
                                ins = dve.scalar_tensor_tensor(out=macc[:, v], in0=w, scalar=silc[:, v, k:k + 1],
                                                               in1=macc[:, v], op0=ALU.mult, op1=ALU.add)
                            ins.then_inc(mod_step, 1)

            def mod_reduce(u, lm, ul):
                dve.wait_ge(mod_tr, u + 1)
                for v in range(2):
                    ins = dve.tensor_reduce(modL[lm][:, bass.ds(4 * ul, 4), v],
                                            ps[:, 6 + v].rearrange("p (a b) -> p a b", a=4), AX.X, ALU.add)
                ins.then_inc(mod_sum, 1)

            def columns(l, sub):
                m, b = modL[l], vecA[:, l]
                need = l * MOD_UNITS + 6 * (sub + 1)
                dve.wait_ge(mod_sum, need)
                post_w = 1.0 if sub == 1 else 0.5
                for v in range(2):
                    for i, part in enumerate((1, 0, 2)):
                        r = slice((3 * sub + part) * KD, (3 * sub + part + 1) * KD)
                        if part == 0:
                            link(dve.tensor_tensor(gcol[:, 1, :, v], m[:, r, v], b[:, r], ALU.add))
                            continue
                        link(dve.tensor_tensor(colt[:, :, v], m[:, r, v], b[:, r], ALU.add))
                        gain = b[:, (VA_PRE if part == 1 else VA_POST) + sub * KD:][:, 0:KD]
                        link(dve.scalar_tensor_tensor(out=gcol[:, i, :, v], in0=colt[:, :, v],
                                                      scalar=1.0 if part == 1 else post_w, in1=gain,
                                                      op0=ALU.add if part == 1 else ALU.mult, op1=ALU.mult))

            def inv_std(l, sub, post, n):
                a, w = halves_of(l, sub, post)[n]
                e = stat_event(l, sub, post, n)
                dve.wait_ge(std_done, e + 1)
                if post:
                    dve.wait_ge(xr_done, KD * (pre_event(l, sub, 1) + 1))
                elif (l, sub) != (0, 0):
                    dve.wait_ge(yr_done, KD * pre_event(l, sub, 0))
                if n == 1:
                    dve.wait_ge(yr_done if post else xr_done, KD * pre_event(l, sub, 1))
                dve.reciprocal(rstd[:, 0:w], ps[:, 6 + n, 0:w]).then_inc(rstd_done, 1)
                dve.wait_ge(rstd_done, e + 1)

            def pre(l, sub, n):
                a, w = halves_of(l, sub, 0)[n]
                hn = hn_of(sub)
                p = pre_event(l, sub, n)
                inv_std(l, sub, 0, n)
                if (l, sub) != (0, 0):
                    dve.wait_ge(unit_done, units_before(mix_tile0(l) if sub == 1 else ffn_tile0(l, sub // 2)))

                def norm(k):
                    if k >= 3:
                        dve.wait_ge(hlo_done, KD * p + k - 2)
                    dve.tensor_tensor(tmp3[k % 3][:, 0:w], xT[:, k, a:a + w], rstd[:, 0:w], ALU.mult
                                      ).then_inc(xr_done, 1)

                def modulate(k):
                    dve.wait_ge(xr_done, KD * p + k + 1)
                    for s, sw, v in segments(a, w):
                        t = tmp3[k % 3][:, s - a:s - a + sw]
                        ins = dve.tensor_scalar(t, t, gcol[:, 0, k, v:v + 1], gcol[:, 1, k, v:v + 1],
                                                ALU.mult, ALU.add)
                    ins.then_inc(hn_done, 1)

                def low(k):
                    dve.wait_ge(hhi_done, KD * p + k + 1)
                    dve.tensor_tensor(hn[:, 1, k, a:a + w], tmp3[k % 3][:, 0:w], hn[:, 0, k, a:a + w].bitcast(F32),
                                      ALU.subtract).then_inc(hlo_done, 1)

                for k in range(KD + 2):
                    if k < KD:
                        norm(k)
                    if 1 <= k <= KD:
                        modulate(k - 1)
                    if k >= 2:
                        low(k - 2)

            def post(l, sub, n):
                a, w = halves_of(l, sub, 1)[n]
                y = y_of(sub)
                r = post_event(l, sub, n)
                inv_std(l, sub, 1, n)

                def norm(k):
                    if k >= 3:
                        dve.wait_ge(x_done, KD * r + k - 2)
                    dve.tensor_tensor(tmp3[k % 3][:, 0:w], y[:, k, a:a + w], rstd[:, 0:w], ALU.mult
                                      ).then_inc(yr_done, 1)

                def add(k):
                    dve.wait_ge(yr_done, KD * r + k + 1)
                    for s, sw, v in segments(a, w):
                        ins = dve.scalar_tensor_tensor(out=xT[:, k, s:s + sw], in0=tmp3[k % 3][:, s - a:s - a + sw],
                                                       scalar=gcol[:, 2, k, v:v + 1], in1=xT[:, k, s:s + sw],
                                                       op0=ALU.mult, op1=ALU.add)
                    ins.then_inc(x_done, 1)

                for k in range(KD + 1):
                    if k < KD:
                        norm(k)
                    if k >= 1:
                        add(k - 1)

            def down_evac(d, unit, dt, first, hv, y, n):
                a, w = hv[n]
                dve.wait_ge(unit_done, unit)
                dst = y[:, dt, a:a + w]
                src = ps[:, 4 + n, 0:w]
                if first:
                    dve.tensor_copy(dst, src).then_inc(yadd_done, 1)
                else:
                    dve.wait_ge(yadd_done, d - DOWN_OUT + 3)
                    dve.tensor_tensor(dst, src, dst, ALU.add).then_inc(yadd_done, 1)

            def ffn(l, j):
                t0, q0, d0 = ffn_tile0(l, j), ffn_pair0(l, j), ffn_down0(l, j)
                hv = halves_of(l, 2 * j, 1)
                for g, (c0, G) in enumerate(GROUPS):
                    u0 = mod_unit0(l, j, g)
                    lm, ul = (u0 // MOD_UNITS, u0 % MOD_UNITS) if u0 is not None else (0, 0)

                    def up_body(i, last):
                        for b in range(2):
                            t = t0 + 4 * i + 2 * b
                            q = q0 + 4 * i + 2 * b
                            s, kc = 2 * b, 2 * i + b
                            used = units_before(t0) + 8 * i + 4 * b + 2
                            if u0 is not None:
                                mod_tiles(u0 + i, (2 * b, 2 * b + 1))
                            w_lo(t + 2, (s + 2) % RAW, 0)
                            for n, (a, w) in enumerate(hv):
                                dve.wait_ge(unit_done, used + n + 1)
                                dve.wait_ge(silu_done, q + n + 3)
                                dve.wait_ge(alo_done, q + n + 1)
                                dve.tensor_tensor(af2[n][:, 0:w], ps[:, 2 + n, 0:w], sg2[n][:, 0:w], ALU.mult
                                                  ).then_inc(amul_done, 1)
                                dve.wait_ge(ahi_done, q + n + 1)
                                lo = OVER if last and b == 1 else 0
                                dve.tensor_tensor(aT[lo:P, 1, kc, a:a + w], af2[n][lo:P, 0:w],
                                                  aT[lo:P, 0, kc, a:a + w].bitcast(F32), ALU.subtract
                                                  ).then_inc(alo_done, 1)
                            w_lo(t + 3, (s + 3) % RAW, 1)
                        if u0 is not None:
                            mod_reduce(u0 + i, lm, ul + i)

                    if g == len(GROUPS) - 1:
                        dve.wait_ge(unit_done, units_before(t0))
                        for half in range(2):
                            ins = dve.memset(aT[0:OVER, half, G - 1].bitcast(F32), 0.0)
                        ins.then_inc(pad_done, 1)
                    n_loop = G // 2 - (g == len(GROUPS) - 1)
                    with dve.Fori(0, n_loop) as i:
                        up_body(i, False)
                    if n_loop < G // 2:
                        up_body(n_loop, True)
                    t0 += 2 * G
                    q0 += 2 * G
                    if u0 is not None:
                        u0, ul = u0 + G // 2, ul + G // 2

                    def down_body(i):
                        for s in range(4):
                            t, d = t0 + 4 * i + s, d0 + 8 * i + 2 * s
                            unit = units_before(t0) + 8 * i + 2 * s + 1
                            down_evac(d, unit, 4 * i + s, g == 0, hv, yF, 0)
                            if u0 is not None:
                                mod_tiles(u0 + i, (s,))
                            down_evac(d + 1, unit + 1, 4 * i + s, g == 0, hv, yF, 1)
                            if isinstance(t, int) and t + CONV >= ALL_TILES:
                                continue
                            w_lo(t + 2, (s + 2) % RAW, s % 2)
                        if u0 is not None:
                            mod_reduce(u0 + i, lm, ul + i)

                    if l == L - 1 and j == 1 and g == len(GROUPS) - 1:
                        for i in range(KD // 4):
                            down_body(i)
                    else:
                        with dve.Fori(0, KD // 4) as i:
                            down_body(i)
                    t0 += KD
                    d0 += DOWN_OUT

            def mixer(l):
                t0 = mix_tile0(l)
                fb = 2 * N_FEAT * l
                fh, oh = full_halves(l), out_halves(l)

                def lo_after(i):
                    t = t0 + i
                    w_lo(t + 2, (t + 2) % RAW, t % 2)

                for i in range(4):
                    lo_after(i)
                dve.wait_ge(tab_in, 16 * (l + 1))
                for n, (a, w) in enumerate(fh):
                    dve.wait_ge(sel_done, 8 * l + 4 + n + 1)
                    dve.tensor_tensor(krT[:, a:a + w], ps[:, 6 + n, 0:w], cosT[:, 0, a:a + w], ALU.mult
                                      ).then_inc(kro_out, 1)
                for n, (a, w) in enumerate(fh):
                    dve.wait_ge(sel_done, 8 * l + 6 + n + 1)
                    link(dve.tensor_tensor(krt[:, n, 0:w], ps[:, 6 + n, 0:w], cosT[:, 1, a:a + w], ALU.mult))
                    dve.tensor_tensor(krT[:, a:a + w], krT[:, a:a + w], krt[:, n, 0:w], ALU.add
                                      ).then_inc(kro_out, 1)
                dve.wait_ge(gates_out, 4 * (l + 1))
                dve.scalar_tensor_tensor(out=rT, in0=rX, scalar=-1.0, in1=rX, op0=ALU.mult, op1=ALU.min
                                         ).then_inc(nabs_done, 1)
                for i, (src, dst, r2, gain, halves) in enumerate((
                        (ckv, ckn, 0, VB_KVN, fh), (cq[:, 0], cqn[:, :, 0], 1, VB_QN, oh),
                        (cq[:, 1], cqn[:, :, 1], 1, VB_QN + 1, oh))):
                    for n, (a, w) in enumerate(halves):
                        if i < 2:
                            dve.wait_ge(lstd_done, 4 * l + 2 * i + n + 1)
                            link(dve.reciprocal(rstd2[r2][:, a:a + w], rstd2[r2][:, a:a + w]))
                        v = src[:, a:a + w]
                        link(dve.scalar_tensor_tensor(out=v, in0=v, scalar=vecB[:, l, gain:gain + 1],
                                                      in1=rstd2[r2][:, a:a + w], op0=ALU.mult, op1=ALU.mult))
                        link(dve.tensor_copy(dst[:, 0, a:a + w], v))
                        dve.tensor_tensor(dst[:, 1, a:a + w], v, dst[:, 0, a:a + w].bitcast(F32), ALU.subtract
                                          ).then_inc(lat_done, 1)
                    lo_after(4 + i)
                lo_after(7)
                for tt in range(NT):
                    dve.wait_ge(unit_done, unit_of(l, 7, tt))
                    dve.tensor_copy(vext[:, tt, :, 0:MDH], ps[:, tt].rearrange("p (h e) -> p h e", h=MH)
                                    ).then_inc(v_out, 1)
                dve.wait_ge(lnf_done, l + 1)
                link(dve.scalar_tensor_tensor(out=rT, in0=rX, scalar=0.0, in1=rT, op0=ALU.min, op1=ALU.subtract))

                def scans(dst, src, op, post_op):
                    link(dve.tensor_tensor_scan(dst[0:32], src[0:32], src[0:32], 0.0, op, post_op))
                    back = slice(None, None, -1)
                    link(dve.tensor_tensor_scan(dst[32:GROW, 0:CTX][:, back], src[32:GROW, 0:CTX][:, back],
                                                src[32:GROW, 0:CTX][:, back], 0.0, op, post_op))
                    link(dve.tensor_tensor_scan(dst[32:GROW, CTX:T][:, back], src[32:GROW, CTX:T][:, back],
                                                src[32:GROW, CTX:T][:, back], dst[32:GROW, 0:1], op, post_op))

                scans(rB, rT, ALU.add, ALU.bypass)
                link(dve.tensor_tensor(rI, rI, rB, ALU.subtract))
                scans(rX, rI, ALU.max, ALU.max)
                link(dve.scalar_tensor_tensor(out=rB, in0=rB, scalar=-1.0, in1=rX, op0=ALU.mult, op1=ALU.subtract))
                dve.tensor_scalar(negG[0:GROW], rX, -1.0, None, ALU.mult).then_inc(rows_done, 1)
                for n in range(KD):
                    dve.wait_ge(cmid_done, KD * l + n + 1)
                    u, out_, wt = qkT[:, n], cv[n % 2], vecB[:, l]
                    streams = ((0, CTX), (CTX, SEQ)) if l < L - 1 or n >= MH else ((CTX, SEQ),)
                    for a, w in streams:
                        dve.scalar_tensor_tensor(out=out_[:, a + 1:a + w], in0=u[:, a:a + w - 1],
                                                 scalar=wt[:, VB_CW + n:VB_CW + n + 1], in1=out_[:, a + 1:a + w],
                                                 op0=ALU.mult, op1=ALU.add).then_inc(dchain, 1)
                        chain[0] += 1
                    dve.wait_ge(dchain, chain[0])
                    for a, w in streams:
                        ins = dve.scalar_tensor_tensor(out=out_[:, a:a + w - 1], in0=u[:, a + 1:a + w],
                                                       scalar=wt[:, VB_CW + 2 * KD + n:VB_CW + 2 * KD + n + 1],
                                                       in1=out_[:, a:a + w - 1], op0=ALU.mult, op1=ALU.add)
                    ins.then_inc(ctap_done, 1)
                    lo_after(8 + n)
                dve.wait_ge(rtr_done, 2 * l + 1)
                dve.tensor_copy(colF[:].rearrange("p a b -> p (a b)"), ps[:, 6, 0:NT * GROW]).then_inc(colF_done, 1)
                for i in range(16, 24):
                    lo_after(i)
                for z in range(2):
                    for n, (a, w) in enumerate(oh):
                        dve.wait_ge(sw_done, 4 * l + 2 * z + n + 1)
                        dve.wait_ge(feat_out, fb + 2 * (20 + z) + n + 1)
                        q = qrT[:, z, a:a + w]
                        link(dve.tensor_tensor(q, ps[:, 6 + n, 0:w], cosT[:, 1, a:a + w], ALU.mult))
                        link(dve.tensor_tensor(tmpq[:, 0:w], cv[z][:, a:a + w], cosT[:, 0, a:a + w], ALU.mult))
                        dve.tensor_tensor(q, q, tmpq[:, 0:w], ALU.add).then_inc(qr_out, 1)
                items = attn_items(l)
                a0 = items_before(l)
                for i in range(len(items) + 2):
                    if i < len(items):
                        h, tt = items[i]
                        dve.wait_ge(sc_done, a0 + i + 1)
                        b = 2 * (i % 2)
                        src = ps[:, b:b + 2, 0:HW] if tt >= NTC else ps[:, b, 0:CTX]
                        link(dve.tensor_reduce(stat[:, 0, i % 8:i % 8 + 1], src,
                                               AX.XY if tt >= NTC else AX.X, ALU.max))
                        dve.tensor_scalar(stat[:, 0, i % 8:i % 8 + 1], stat[:, 0, i % 8:i % 8 + 1], -SM_SCALE, None,
                                          ALU.mult).then_inc(max_done, 1)
                    if 1 <= i <= len(items) and items[i - 1][1] >= NTC:
                        h, tt = items[i - 1]
                        dve.wait_ge(pt_done, a0 + i)
                        if i - 1 >= 2:
                            dve.wait_ge(pv_done, a0 + i - 2)
                        dve.tensor_copy(ptb[:, (i - 1) % 2, 4:6].rearrange("p a b -> p (a b)"), ps[:, 5, 0:2 * P]
                                        ).then_inc(ptd_out, 1)
                    if i >= 2:
                        h, tt = items[i - 2]
                        k = (i - 2) % 8
                        dve.wait_ge(exp_done, a0 + i - 1)
                        link(dve.reciprocal(stat[:, 1, 8 + k:9 + k], stat[:, 1, k:k + 1]))
                        dve.wait_ge(pv_done, a0 + i - 1)
                        dve.tensor_scalar(atok[:, tt, h * VD:(h + 1) * VD], ps[:, 6 + (i - 2) % 2, 0:VD],
                                          stat[:, 1, 8 + k:9 + k], None, ALU.mult).then_inc(pv_out, 1)
                for h in range(MH + 1):
                    for j in range(NT if h < MH else 0):
                        for d in range(2):
                            diag, rest = source_blocks(l, d, j)
                            if diag is None:
                                continue
                            i = block_index(l, h, j, d)
                            s = slice(diag * P, (diag + 1) * P)
                            dve.wait_ge(g_out, 4 * (MH * l + h) + 2 * d + 2)
                            if i >= 2:
                                dve.wait_ge(pb_done, i - 1)
                            dve.scalar_tensor_tensor(
                                out=dbuf[:, d, s], in0=gbc[:, d, s],
                                scalar=colF[:, j, 32 * d + h:32 * d + h + 1],
                                in1=cst[:, C_MF + d * P:C_MF + (d + 1) * P], op0=ALU.add, op1=ALU.min
                            ).then_inc(dg_done, 1)
                        for d in range(2):
                            i = block_index(l, h, j, d)
                            dve.wait_ge(dx_done, i + 1)
                            dve.wait_ge(s_done, NT * (MH * l + h) + j + 1)
                            if h >= 2:
                                dve.wait_ge(mo_done, OUT_UNITS * l + 4 * (h - 1))
                            for slot, a, w in product_ranges(l, d, j):
                                src = ps[:, 4, j * CTX + a:j * CTX + a + w] if a < CTX else \
                                    ps[:, 2 + j % 2, a - CTX:a - CTX + w]
                                ins = dve.scalar_tensor_tensor(
                                    out=pblk[:, h % 2, d, slot:slot + w // P].rearrange("p a b -> p (a b)"),
                                    in0=src, scalar=K_SCALE, in1=dbuf[:, d, a:a + w], op0=ALU.mult, op1=ALU.mult)
                            ins.then_inc(pb_done, 1)
                    if h >= 1:
                        mlstm_out(l, h - 1)
                tts = o_tts(l)
                t1 = tts[0]
                rs = stat[:, 2, 0:NT * MH].rearrange("p (h t) -> p h t", h=MH)[:, :, t1:NT]
                link(dve.tensor_copy(rs, mv[:, :, 1].rearrange("p (h t) -> p h t", h=MH)[:, :, t1:NT]))
                dve.wait_ge(pv_out, a0 + len(items))
                for tt in tts:
                    ins = dve.tensor_tensor_reduce(out=sqw, in0=atok[:, tt], in1=atok[:, tt], scale=1.0, scalar=0.0,
                                                   op0=ALU.mult, op1=ALU.add, accum_out=stat[:, 3, tt:tt + 1])
                    if tt < tts[-1]:
                        link(ins)
                    else:
                        ins.then_inc(fvar_done, 1)
                dve.wait_ge(fstd_done, 2 * (l + 1))
                link(dve.reciprocal(rs, rs))
                link(dve.reciprocal(stat[:, 3, t1:NT], stat[:, 3, t1:NT]))
                for tt in tts:
                    dve.tensor_scalar(atok[:, tt], atok[:, tt], stat[:, 3, tt:tt + 1], None, ALU.mult
                                      ).then_inc(fin_done, 1)
                for h in range(MH):
                    for tt in tts:
                        k = h * NT + tt
                        v = otok[:, tt, h * MDH:(h + 1) * MDH]
                        dve.tensor_scalar(v, v, mv[:, k, 0:1], stat[:, 2, k:k + 1], ALU.subtract, ALU.mult
                                          ).then_inc(fin_done, 1)
                for cidx in range(KD):
                    for n, (a, w) in enumerate(oh):
                        i = 16 * l + 2 * cidx + n
                        dve.wait_ge(mhi_done, i + 1)
                        dve.scalar_tensor_tensor(out=mixT[:, 1, cidx, a:a + w], in0=ps[:, (2 * cidx + n) % 4, 0:w],
                                                 scalar=vecB[:, l, VB_AN + cidx:VB_AN + cidx + 1],
                                                 in1=mixT[:, 0, cidx, a:a + w].bitcast(F32),
                                                 op0=ALU.mult, op1=ALU.subtract).then_inc(mlo_done, 1)
                for i in range(KD):
                    for n in range(2):
                        down_evac(out_down0(l) + 2 * i + n, unit_of(l, WOUT_TILE + i, n), i, True, oh, yM, n)
                    lo_after(24 + i)

            def mlstm_out(l, h):
                for d in range(2):
                    for z, tts in enumerate(triples(l)):
                        o = OUT_UNITS * l + 4 * h + 2 * d + z
                        n = len(tts)
                        W = MDH + 1
                        bank = ps[:, 5 + o % 3, 0:n * W].rearrange("p (t e) -> p t e", e=W)
                        r = 32 * d + h
                        dve.wait_ge(mo_done, o + 1)
                        if o >= 1:
                            dve.wait_ge(mo_out, o)
                        link(dve.tensor_copy(dn[:, 1, 0:n], bank[:, :, MDH]))
                        link(dve.scalar_tensor_tensor(out=dn[:, 0, 0:n], in0=dn[:, 1, 0:n], scalar=-1.0,
                                                      in1=dn[:, 1, 0:n], op0=ALU.mult, op1=ALU.max))
                        link(dve.tensor_tensor(dn[:, 0, 0:n], dn[:, 0, 0:n], expnm[:, tts[0]:tts[0] + n, r],
                                               ALU.max))
                        link(dve.reciprocal(dn[:, 1, 0:n], dn[:, 0, 0:n]))
                        den = dn[:, 1, 0:n].unsqueeze(2).broadcast_to([P, n, MDH])
                        dst = hh[:, tts[0]:tts[0] + n]
                        if d == 0:
                            dve.tensor_tensor(dst, bank[:, :, 0:MDH], den, ALU.mult).then_inc(mo_out, 1)
                        else:
                            dve.tensor_tensor(ht[:, 0:n], bank[:, :, 0:MDH], den, ALU.mult).then_inc(mo_out, 1)
                            dve.wait_ge(mo_out, o + 1)
                            link(dve.tensor_tensor(dst, dst, ht[:, 0:n], ALU.add))
                tts = o_tts(l)
                g = otok[:, tts[0]:NT, h * MDH:(h + 1) * MDH]
                dve.wait_ge(o_outs, o_before(l) + len(tts))
                link(dve.tensor_tensor(g, g, hh[:, tts[0]:NT], ALU.mult))
                for i, tt in enumerate(tts):
                    link(dve.bn_stats(bn6[:, i % 2], otok[:, tt, h * MDH:(h + 1) * MDH]))
                    link(dve.bn_aggr(mv[:, h * NT + tt], bn6[:, i % 2]))

            link(dve.memset(epsc, EPS))
            link(dve.memset(onec, 1.0))
            dve.memset(zeroc, 0.0).then_inc(wlo_done, RAW)
            dve.memset(kc[:, 3:4], 0.0).then_inc(amul_done, 2)
            dve.wait_ge(amul_done, 2)
            dve.memset(kc[:, 3:4], 0.0).then_inc(yadd_done, 2)
            dve.wait_ge(yadd_done, 2)
            dve.memset(kc[:, 3:4], 0.0).then_inc(alo_done, 2)
            for i in range(4):
                n = VA_N if i % 2 == 0 else VB_N
                dve.wait_ge(vtr, i + 1)
                dst = (vecA if i % 2 == 0 else vecB)[:, i // 2]
                dve.tensor_copy(dst, ps[:, i, 0:n]).then_inc(vev, 1)
            for i in range(2 * KD):
                dve.wait_ge(xtr, i + 1)
                k, n = i // 2, i % 2
                dve.tensor_copy(xT[:, k, n * HW:(n + 1) * HW], ps[:, i % 6, 0:HW]).then_inc(xev, 1)
            dve.wait_ge(silu_done, 2)
            mod_tiles(0, range(4))
            mod_reduce(0, 0, 0)
            with dve.Fori(1, FIRST_UNITS) as i:
                mod_tiles(i, range(4))
                mod_reduce(i, 0, i)
            for t in range(CONV):
                w_lo(t, t, t)
            for l in range(L):
                for sub in range(3):
                    columns(l, sub)
                    for n in range(2):
                        pre(l, sub, n)
                    if sub == 1:
                        mixer(l)
                    else:
                        ffn(l, sub // 2)
                    for n in range(2):
                        post(l, sub, n)
            for i in range(2 * (SEQ // P)):
                dve.wait_ge(otr, i + 1)
                if i >= 4:
                    dve.wait_ge(o_out[(i // 2) % 2], 16 * (i // 4))
                dve.tensor_copy(ostage[:, (i // 2) % 2, (i % 2) * 512:(i % 2 + 1) * 512], ps[:, i % 4]
                                ).then_inc(oev, 1)

        @block.tensor
        def _(pe):
            def three(dst, w, x, first, last):
                pe.matmul(dst, w(0), x(0), start=first, stop=False)
                pe.matmul(dst, w(0), x(1), start=False, stop=False)
                return pe.matmul(dst, w(1), x(0), start=False, stop=last)

            def weight(cs, at, width=P):
                return lambda p: wsp[:, cs, p, at:at + width]

            def stats(l, sub, post, n):
                a, w = halves_of(l, sub, post)[n]
                e = stat_event(l, sub, post, n)
                if e >= 2:
                    pe.wait_ge(rstd_done, e - 1)
                for k in range(KD):
                    pe.wait_ge(sq_done, KD * e + k + 1)
                    pe.matmul(ps[:, 6 + n, 0:w], ones, sq2[k % 2][:, 0:w], start=k == 0, stop=k == KD - 1
                              ).then_inc(stat_mm, 1)

            def mod_turn(u):
                pe.wait_ge(mod_step, 16 * u + 16)
                if not (isinstance(u, int) and u == 0):
                    pe.wait_ge(mod_sum, u)
                for v in range(2):
                    for b in range(4):
                        ins = pe.transpose(ps[:, 6 + v, b * P:(b + 1) * P], macc[:, v, b * P:(b + 1) * P], ident)
                ins.then_inc(mod_tr, 1)

            def down_tile(t, cs, d, G, hv, x, ready=None):
                pe.wait_ge(wlo_done, t + 1 + RAW)
                for n, (a, w) in enumerate(hv):
                    pe.wait_ge(yadd_done, d + n + 1)
                    for k in range(G):
                        if ready is not None:
                            ready(n, k)
                        ins = three(ps[:, 4 + n, 0:w], weight(cs, k * P), lambda p: x[:, p, k, a:a + w],
                                    k == 0, k == G - 1)
                    ins.then_inc(unit_done, 1)

            def ffn(l, j):
                t0, q0, d0 = ffn_tile0(l, j), ffn_pair0(l, j), ffn_down0(l, j)
                hv = halves_of(l, 2 * j, 1)
                hin = halves_of(l, 2 * j, 0)
                assert hv == hin
                for g, (c0, G) in enumerate(GROUPS):
                    u0 = mod_unit0(l, j, g)

                    def up_body(i):
                        for b in range(2):
                            t = t0 + 4 * i + 2 * b
                            q = q0 + 4 * i + 2 * b
                            for wi, freed in ((0, silu_done), (1, amul_done)):
                                pe.wait_ge(wlo_done, t + wi + 1 + RAW)
                                for n, (a, w) in enumerate(hv):
                                    pe.wait_ge(hlo_done, KD * (pre_event(l, 2 * j, n) + 1))
                                    pe.wait_ge(freed, q + n + 1)
                                    for k in range(KD):
                                        ins = three(ps[:, 2 * wi + n, 0:w], weight(wi, k * P),
                                                    lambda p: hnF[:, p, k, a:a + w], k == 0, k == KD - 1)
                                    ins.then_inc(unit_done, 1)
                        if u0 is not None:
                            mod_turn(u0 + i)

                    n_loop = G // 2 - (g == len(GROUPS) - 1)
                    with pe.Fori(0, n_loop) as i:
                        up_body(i)
                    if n_loop < G // 2:
                        up_body(n_loop)
                    t0 += 2 * G
                    q0 += 2 * G
                    if u0 is not None:
                        u0 += G // 2

                    def down_body(i):
                        def ready(n, k):
                            if k == 0:
                                pe.wait_ge(alo_done, q0)
                                if g == len(GROUPS) - 1:
                                    pe.wait_ge(pad_done, 2 * l + j + 1)
                            if k == G - 1:
                                pe.wait_ge(alo_done, q0 + 2)
                        for s in range(4):
                            down_tile(t0 + 4 * i + s, s % 2, d0 + 8 * i + 2 * s, G, hv, aT, ready if s == 0 else None)
                        if u0 is not None:
                            mod_turn(u0 + i)

                    with pe.Fori(0, KD // 4) as i:
                        down_body(i)
                    t0 += KD
                    d0 += DOWN_OUT

            def mixer(l):
                t0 = mix_tile0(l)
                fb = 2 * N_FEAT * l
                fh, oh = full_halves(l), out_halves(l)

                def split(i):
                    pe.wait_ge(wlo_done, t0 + i + 1 + RAW)
                    return (t0 + i) % 2

                def feature(f, cs, K, wat, x, halves, step=P):
                    for n, (a, w) in enumerate(halves):
                        for k in range(K):
                            ins = three(ps[:, 2 * (f % 2) + n, 0:w], weight(cs, wat + k * step),
                                        lambda p: x(p, k, a, w), k == 0, k == K - 1)
                        ins.then_inc(unit_done, 1)

                def hn(p, k, a, w):
                    return hnM[:, p, k, a:a + w]

                def small(z, lhsT, rhs, halves, rows_=P):
                    for n, (a, w) in enumerate(halves):
                        pe.matmul(ps[0:rows_, 6 + n, 0:w], lhsT, rhs[:, a:a + w], start=True, stop=True
                                  ).then_inc(sel_done, 1)

                def lat_stat(i, src, halves, first, last):
                    for n, (a, w) in enumerate(halves):
                        pe.wait_ge(lsq_done, 6 * l + 2 * i + n + 1)
                        pe.matmul(ps[:, 6 + n, 0:w], ones, sq2[n][:, 0:w], start=first, stop=last
                                  ).then_inc(lstat_done, 1)

                def token_major(i, j, tts, width, freed):
                    cs = split(i)
                    for tt in tts:
                        if j == 0:
                            freed(tt)
                        for k in range(2):
                            ins = three(ps[:, tt, 0:width], lambda p: hnM[:, p, 2 * j + k, tt * P:(tt + 1) * P],
                                        lambda p: wsp[:, cs, p, k * MW:(k + 1) * MW], j == 0 and k == 0,
                                        j == 3 and k == 1)
                        if j == 3 or tt == tts[-1]:
                            ins.then_inc(unit_done, 1)

                for n in range(2):
                    pe.wait_ge(hlo_done, KD * (pre_event(l, 1, n) + 1))
                feature(0, split(0), KD, 0, hn, fh)
                feature(1, split(1), KD, 0, hn, fh)
                pe.wait_ge(feat_out, fb + 2)
                pe.wait_ge(rstd_done, stat_event(l, 1, 0, 1) + 1)
                small(0, cst[:, C_SELI:C_SELI + GROW], krg, fh, GROW)
                cs = split(2)
                feature(2, cs, KD, 0, hn, oh)
                pe.wait_ge(gates_out, 4 * l + 2)
                small(1, cst[:, C_SELF:C_SELF + GROW], krg, fh, GROW)
                pe.wait_ge(feat_out, fb + 4)
                cs = split(3)
                feature(3, cs, KD, 0, hn, oh)
                pe.wait_ge(gates_out, 4 * l + 4)
                small(2, cst[:, C_KD:C_KD + P], krg, fh)

                def v_free(tt):
                    pe.wait_ge(feat_out, fb + 8)
                    pe.wait_ge(yadd_done, ffn_down0(l, 0) + DOWN_FFN + 2)

                token_major(4, 0, range(NT), MW, v_free)
                pe.wait_ge(kro_out, 4 * l + 2)
                small(3, cst[:, C_KSW:C_KSW + P], krg, fh)
                pe.wait_ge(kro_out, 4 * l + 4)
                lat_stat(0, ckv, fh, True, True)
                token_major(5, 1, range(NT), MW, None)
                pe.wait_ge(lstd_done, 4 * l + 2)
                lat_stat(1, cq[:, 0], oh, True, False)
                lat_stat(2, cq[:, 1], oh, False, True)
                token_major(6, 2, range(NT), MW, None)
                token_major(7, 3, range(NT), MW, None)
                for n in range(KD):
                    f = 4 + n
                    cs = split(8 + n)
                    if n < 2:
                        pe.wait_ge(v_out, NT * l + 2 * (n + 1))
                    else:
                        pe.wait_ge(feat_out, fb + 2 * (f - 1))
                    feature(f, cs, KD, 0, hn, oh if n < MH else fh)
                    if n == 4:
                        pe.wait_ge(rows_done, l + 1)
                        pe.wait_ge(lstd_done, 4 * l + 4)
                        for src, bank in ((rI, 6), (rB, 7)):
                            for tt in range(NT):
                                ins = pe.transpose(ps[:, bank, tt * GROW:(tt + 1) * GROW], src[:, tt * P:(tt + 1) * P],
                                                   ident[0:GROW, 0:GROW])
                            ins.then_inc(rtr_done, 1)

                def o_free(tt):
                    pe.wait_ge(feat_out, fb + 24)
                    pe.wait_ge(v_out, NT * (l + 1))

                for j in range(4):
                    token_major(16 + j, j, o_tts(l), MW, o_free)
                pe.wait_ge(lat_done, 6 * (l + 1))
                cs = split(20)
                for h in range(HEADS):
                    if h == 0:
                        pe.wait_ge(o_outs, o_before(l) + len(o_tts(l)))
                    else:
                        pe.wait_ge(feat_out, fb + 2 * (12 + h - 1))
                    feature(12 + h, cs, 1, h * P, lambda p, k, a, w: ckn[:, p, a:a + w], fh)
                cs = split(21)
                pe.wait_ge(feat_out, fb + 32)
                for tt in range(NT):
                    three(ps[:, tt], lambda p: ckn[:, p, tt * P:(tt + 1) * P], weight(cs, 0, HEADS * P), True, True
                          ).then_inc(unit_done, 1)
                cs = split(22)
                for h in range(HEADS):
                    if h < 2:
                        pe.wait_ge(va_out, NT * l + 2 * (h + 1))
                    else:
                        pe.wait_ge(feat_out, fb + 2 * (16 + h - 1))
                    feature(16 + h, cs, 2, h * P, lambda p, k, a, w: cqn[:, p, k, a:a + w], oh, HEADS * NOPE)
                cs = split(23)
                for z in range(2):
                    pe.wait_ge(feat_out, fb + 2 * (20 + z - 1))
                    feature(20 + z, cs, 2, z * P, lambda p, k, a, w: cqn[:, p, k, a:a + w], oh, HEADS * ROPE)
                pe.wait_ge(colF_done, l + 1)
                pe.wait_ge(expnm_done, l + 1)
                for z in range(2):
                    for n, (a, w) in enumerate(oh):
                        pe.wait_ge(feat_out, fb + 2 * (20 + z) + n + 1)
                        if z == 1:
                            pe.wait_ge(qr_out, 4 * l + n + 1)
                        pe.matmul(ps[:, 6 + n, 0:w], cst[:, C_SWQ:C_SWQ + P], cv[z][:, a:a + w], start=True, stop=True
                                  ).then_inc(sw_done, 1)
                items = attn_items(l)
                a0 = items_before(l)
                pe.wait_ge(va_out, NT * (l + 1))

                def scores(i):
                    h, tt = items[i]
                    if i >= 2:
                        pe.wait_ge(exp_done, a0 + i - 1)
                    q = 64 * (h % 2)
                    for b in range(2 if tt >= NTC else 1):
                        ks = slice(b * HW, (b + 1) * HW) if tt >= NTC else slice(0, CTX)
                        dst = ps[:, 2 * (i % 2) + b, 0:ks.stop - ks.start]
                        pe.matmul(dst, qnT[:, h, tt * P:(tt + 1) * P], knT[:, h, ks], start=True, stop=False)
                        ins = pe.matmul(dst, qrT[q:q + 64, h // 2, tt * P:(tt + 1) * P], krT[q:q + 64, ks],
                                        start=False, stop=True)
                    ins.then_inc(sc_done, 1)

                def turn(i):
                    h, tt = items[i]
                    pe.wait_ge(exp_done, a0 + i + 1)
                    if i >= 1:
                        pe.wait_ge(pta_out, a0 + i)
                        if turned_by_dve(l, i - 1) > 0:
                            pe.wait_ge(ptd_out, turned_by_dve(l, i - 1))
                    for s in range(NT if tt >= NTC else NTC):
                        ins = pe.transpose(ps[:, 4 + s // 4, (s % 4) * P:(s % 4 + 1) * P],
                                           pbuf[:, i % 2, s * P:(s + 1) * P], ident)
                    ins.then_inc(pt_done, 1)

                def values(i):
                    h, tt = items[i]
                    pe.wait_ge(pta_out, a0 + i + 1)
                    if tt >= NTC:
                        pe.wait_ge(ptd_out, turned_by_dve(l, i))
                    if i >= 2:
                        pe.wait_ge(pv_out, a0 + i - 1)
                    ns = NT if tt >= NTC else NTC
                    for s in range(ns):
                        ins = pe.matmul(ps[:, 6 + i % 2, 0:VD], ptb[:, i % 2, s], va[:, s, h * VD:(h + 1) * VD],
                                        start=s == 0, stop=s == ns - 1)
                    ins.then_inc(pv_done, 1)

                pe.wait_ge(qr_out, 4 * (l + 1))
                scores(0)
                for i in range(len(items) + 1):
                    if i + 1 < len(items):
                        scores(i + 1)
                    if i < len(items):
                        turn(i)
                    if i >= 1:
                        values(i - 1)
                pe.wait_ge(ones_done, l + 1)

                def head_scores(h):
                    for d in range(2):
                        for z, (a, w) in enumerate(((0, CTX), (CTX, SEQ))):
                            gi = 4 * (MH * l + h) + 2 * d + z
                            if gi >= 2:
                                pe.wait_ge(g_out, gi - 1)
                            row = 32 * d + h
                            pe.matmul(ps[:, z, 0:w], ident[0:GROW, row:row + 1].broadcast_to([GROW, P]), negG[0:GROW, a:a + w],
                                      start=True, stop=True).then_inc(g_done, 1)
                    for j in range(NT):
                        if h > 0 or j >= 2:
                            pe.wait_ge(pb_done, block_index(l, h, j, 0) - 2)
                        if j == 0 and l < L - 1:
                            for jj in range(NTC):
                                pe.matmul(ps[:, 4, jj * CTX:(jj + 1) * CTX], qkT[:, MH + h, jj * P:(jj + 1) * P],
                                          qkT[:, h, 0:CTX], start=True, stop=True)
                        pe.matmul(ps[:, 2 + j % 2, 0:SEQ], qkT[:, MH + h, j * P:(j + 1) * P], qkT[:, h, CTX:T],
                                  start=True, stop=True).then_inc(s_done, 1)

                def head_out(h):
                    for d in range(2):
                        slots = source_slots(l, d)
                        for z, tts in enumerate(triples(l)):
                            o = OUT_UNITS * l + 4 * h + 2 * d + z
                            if o >= 3:
                                pe.wait_ge(mo_out, o - 2)
                            pe.wait_ge(pb_done, block_index(l, h, NT, 0))
                            for m, tt in enumerate(tts):
                                dst = ps[:, 5 + o % 3, m * (MDH + 1):(m + 1) * (MDH + 1)]
                                src = sources_of(d, tt)
                                for j in src:
                                    ins = pe.matmul(dst, pblk[:, h % 2, d, slots[j, tt]], vext[:, j, h],
                                                    start=j == src[0], stop=j == src[-1])
                            ins.then_inc(mo_done, 1)

                pe.wait_ge(conv_done, KD * (l + 1))
                pe.wait_ge(pv_out, a0 + len(items))
                head_scores(0)
                for h in range(MH):
                    if h + 1 < MH:
                        head_scores(h + 1)
                    head_out(h)
                tts = o_tts(l)
                for cidx in range(KD):
                    for n, (a, w) in enumerate(oh):
                        i = 16 * l + 2 * cidx + n
                        pe.wait_ge(fin_done, fin_before(l) + len(tts) * (1 + max(0, cidx - 3)))
                        if i >= 4:
                            pe.wait_ge(mlo_done, i - 3)
                        src = atok if cidx < HEADS else otok
                        at = (cidx % HEADS) * P
                        for m in range(w // P):
                            ins = pe.transpose(ps[:, (2 * cidx + n) % 4, m * P:(m + 1) * P],
                                               src[:, a // P + m, at:at + P], ident)
                        ins.then_inc(mt_done, 1)
                for i in range(KD):
                    def ready(n, k):
                        if i == 0:
                            pe.wait_ge(mlo_done, 16 * l + 2 * k + n + 1)
                    down_tile(t0 + WOUT_TILE + i, (t0 + i) % 2, out_down0(l) + 2 * i, KD, oh, mixT, ready)

            pe.wait_ge(cst_in, 16)
            pe.wait_ge(vec_in, 16 * 11 * L)
            for i in range(4):
                n = VA_N if i % 2 == 0 else VB_N
                pe.transpose(ps[:, i, 0:n], vstage[0:n, i], ident[0:n, 0:n]).then_inc(vtr, 1)
            pe.wait_ge(x_in, 32)
            pe.wait_ge(vev, 4)
            for i in range(2 * KD):
                if i >= 6:
                    pe.wait_ge(xev, i - 5)
                k, n = i // 2, i % 2
                for m in range(3):
                    ins = pe.transpose(ps[:, i % 6, m * P:(m + 1) * P], xstage[:, 3 * n + m, k * P:(k + 1) * P], ident)
                ins.then_inc(xtr, 1)
            mod_turn(0)
            with pe.Fori(1, FIRST_UNITS) as i:
                mod_turn(i)
            for l in range(L):
                for sub in range(3):
                    if sub == 0:
                        pe.wait_ge(mod_sum, l * MOD_UNITS + FIRST_UNITS)
                    for n in range(2):
                        stats(l, sub, 0, n)
                    if sub == 1:
                        mixer(l)
                    else:
                        ffn(l, sub // 2)
                    if sub == 2:
                        pe.wait_ge(mod_sum, min(L, l + 2) * MOD_UNITS - (0 if l == L - 1 else MOD_UNITS - FIRST_UNITS))
                    if sub == 0:
                        pe.wait_ge(mod_sum, (l + 1) * MOD_UNITS)
                    if sub == 1:
                        pe.wait_ge(mo_out, OUT_UNITS * (l + 1))
                    for n in range(2):
                        stats(l, sub, 1, n)
            for i in range(2 * (SEQ // P)):
                tt, half = NTC + i // 2, i % 2
                pe.wait_ge(x_done, KD * (post_event(L - 1, 2, 1) + 1))
                if i >= 4:
                    pe.wait_ge(oev, i - 3)
                for m in range(4):
                    ins = pe.transpose(ps[:, i % 4, m * P:(m + 1) * P], xT[:, 4 * half + m, tt * P:(tt + 1) * P], ident)
                ins.then_inc(otr, 1)


_INS = ["x", "c", "ctx", "c_ctx", "w_mod", "b_mod", "norm_pre", "norm_post", "ffn_w_gate", "ffn_w_up", "ffn_w_down",
        "w_in", "q_norm", "w_uq", "kv_norm", "w_ukv", "attn_out_norm", "conv_w", "conv_b", "gate_b", "mlstm_norm",
        "w_out"]


def kernel(**inputs):
    import concourse.bacc as bacc
    from concourse.bass_utils import run_bass_kernel_spmd

    nc = bacc.Bacc("TRN2", target_bir_lowering=False, num_devices=1)
    arrays, args = {}, []
    for name in _INS:
        a = np.ascontiguousarray(inputs[name])
        arrays[f"in_{name}"] = a
        args.append(nc.dram_tensor(f"in_{name}", a.shape, mybir.dt.from_np(a.dtype), kind="ExternalInput").ap())
    arrays["in_consts"] = constants()
    args.append(nc.dram_tensor("in_consts", (P, C_N), F32, kind="ExternalInput").ap())
    args.append(nc.dram_tensor("out", (1, SEQ, D), F32, kind="ExternalOutput").ap())
    hybrid_backbone_kernel(nc, *args)
    r = run_bass_kernel_spmd(nc, [arrays], core_ids=[0])
    return r.results[0]["out"]
```

```python
from contextlib import ExitStack

import numpy as np
import concourse.bass as bass
from concourse import mybir

F32 = mybir.dt.float32
F32R = mybir.dt.float32r
ALU = mybir.AluOpType
ACT = mybir.ActivationFunctionType
AX = mybir.AxisListType

P = 128
D = 1024
KD = D // P
SEQ = 512
CTX = 256
T = CTX + SEQ
NT = T // P
NTC = CTX // P
SEQ_TILES = SEQ // P
L = 2
FF = 2752
NMOD = 9
EPS = 1e-6
GRID_W = 64
HEADS = 4
QL, KVL, NOPE, ROPE, VD = 256, 128, 128, 64, 128
SM_SCALE = float((NOPE + ROPE) ** -0.5)
MH, MDH = 4, 128
K_SCALE = float(MDH ** -0.5)
MW = MH * MDH
D_IN = QL + KVL + ROPE + 4 * MW + 4 * MH
IN_CQ, IN_CKV, IN_KR = 0, QL, QL + KVL
IN_QK = IN_KR + ROPE
IN_V = IN_QK + 2 * MW
IN_O = IN_V + MW
IN_END = D_IN

NCH = -(-FF // P)
LAST_F = FF - P
OVER = NCH * P - FF
GROUPS = [(0, 6), (6, 8), (14, 8)]
GMAX = 8
RAW, CONV, MODR, MODR0 = 4, 2, 2, 6
HW = 384

NBM = NMOD * KD
VA_PRE, VA_POST, VA_N = NBM, NBM + 3 * KD, NBM + 6 * KD
VB_CW, VB_CB, VB_QN, VB_KVN, VB_AN, VB_MN, VB_C, VB_CC, VB_N = 0, 24, 32, 34, 35, 39, 43, 51, 59

C_ID = 0
C_ONES = C_ID + P
C_SWQ = C_ONES + P
C_KD = C_SWQ + P
C_KSW = C_KD + P
C_SELI = C_KSW + P
C_SELF = C_SELI + 36
C_MF = C_SELF + 36
C_MB = C_MF + P
C_COS = C_MB + P
C_SIN = C_COS + T
C_N = C_SIN + T
C_PERS = C_COS
GROW = 36
GATE_AT = P - 4 * MH


def constants():
    c = np.zeros((P, C_N), np.float32)
    c[:, C_ID:C_ID + P] = np.eye(P)
    c[:, C_ONES:C_ONES + P] = 1.0 / D
    half = ROPE // 4
    for m in range(P):
        r = m % ROPE
        base = m - r
        lo = (r // half) % 2 == 0
        src = r + half if lo else r - half
        c[base + src, C_SWQ + m] = -1.0 if lo else 1.0
        c[r, C_KD + m] = 1.0
        c[src, C_KSW + m] = -1.0 if lo else 1.0
    for h in range(MH):
        c[GATE_AT + 0 * MH + h, C_SELI + h] = 1.0
        c[GATE_AT + 2 * MH + h, C_SELI + 32 + h] = 1.0
        c[GATE_AT + 1 * MH + h, C_SELF + h] = 1.0
        c[GATE_AT + 3 * MH + h, C_SELF + 32 + h] = 1.0
    s, t = np.arange(P)[:, None], np.arange(P)[None, :]
    c[:, C_MF:C_MF + P] = np.where(s <= t, 0.0, -1e30)
    c[:, C_MB:C_MB + P] = np.where(s >= t, 0.0, -1e30)
    f = np.float32
    inv = f(10000.0) ** (-np.arange(half, dtype=f) / f(half))
    pos = np.arange(SEQ)
    for m in range(P):
        axis, fr = (m % ROPE) // (2 * half), m % half
        p = (pos // GRID_W if axis == 0 else pos % GRID_W).astype(f)
        c[m, C_COS:C_COS + CTX] = 1.0
        c[m, C_COS + CTX:C_COS + T] = np.cos(p * inv[fr])
        c[m, C_SIN + CTX:C_SIN + T] = np.sin(p * inv[fr])
    return c


def full_halves(l):
    return [(0, HW), (HW, HW)]


def out_halves(l):
    return [(0, HW), (HW, HW)] if l < L - 1 else [(CTX, SEQ // 2), (CTX + SEQ // 2, SEQ // 2)]


def halves_of(l, sub, post):
    return full_halves(l) if (sub, post) in ((0, 0), (0, 1), (1, 0)) else out_halves(l)


def segments(start, width):
    out = []
    if start < CTX:
        out.append((start, min(width, CTX - start), 1))
    if start + width > CTX:
        a = max(start, CTX)
        out.append((a, start + width - a, 0))
    return out


HEAD = 4
FFN_TILES = HEAD + 2 * NCH + (len(GROUPS) + 1) * KD
MIX_TILES = HEAD + 24 + 2 * KD
V_TILE, QK_TILE, O_TILE = 2 * HEAD, 2 * HEAD + 4, 2 * HEAD + 12
UKN_TILE, UVA_TILE, UQN_TILE, UQR_TILE, WOUT_TILE = (O_TILE + 4 + i for i in range(5))
PER_LAYER = 2 * FFN_TILES + MIX_TILES
def ffn_tile0(l, j): return l * PER_LAYER + j * (FFN_TILES + MIX_TILES)
def mix_tile0(l): return l * PER_LAYER + FFN_TILES
ALL_TILES = L * PER_LAYER
def tile_units(t):
    for l in range(L):
        i = t - mix_tile0(l)
        if 0 <= i < MIX_TILES:
            if V_TILE <= i < QK_TILE or O_TILE <= i < UKN_TILE:
                return NT if i == QK_TILE - 1 else len(o_tts(l)) if i == UKN_TILE - 1 else 1
            if i < 2 * HEAD or i >= WOUT_TILE:
                return 1
            return {UKN_TILE: 2 * HEADS, UVA_TILE: NT, UQN_TILE: 2 * HEADS, UQR_TILE: 4}.get(i, 2)
        for j in range(2):
            i = t - ffn_tile0(l, j)
            if 0 <= i < FFN_TILES:
                return 1 if i < 2 * HEAD or i >= FFN_TILES - 2 * KD else 2
    return 0
def units_before(t): return sum(tile_units(i) for i in range(t))
def unit_of(l, i, n):
    return units_before(mix_tile0(l) + i) + n + 1
def feat_unit(l, f, n):
    if f < HEAD:
        return unit_of(l, HEAD * n + f, 0)
    if f < 12:
        return unit_of(l, QK_TILE + f - HEAD, n)
    i, f0 = (UKN_TILE, 12) if f < 16 else (UQN_TILE, 16) if f < 20 else (UQR_TILE, 20)
    return unit_of(l, i, 2 * (f - f0) + n)
def feat_seq(f, n): return HEAD * n + f if f < HEAD else 2 * f + n
def feat_bank(f, n):
    return HEAD_BANKS[n][f] if f < HEAD else 2 * (f % 2) + n
HEAD_BANKS = [[0, 2, 4, 5], [1, 3, 0, 2]]
def ffn_pair0(l, j): return 2 * NCH * (2 * l + j)
DOWN_FFN = 2 * KD * len(GROUPS)
DOWN_OUT = 2 * KD
def ffn_down0(l, j): return l * (2 * DOWN_FFN + DOWN_OUT) + j * (DOWN_FFN + DOWN_OUT)
def out_down0(l): return l * (2 * DOWN_FFN + DOWN_OUT) + DOWN_FFN
def last_down0(l, sub):
    return out_down0(l) if sub == 1 else ffn_down0(l, sub // 2) + DOWN_FFN - DOWN_OUT
def last_tile0(l, sub):
    return mix_tile0(l) + WOUT_TILE if sub == 1 else ffn_tile0(l, sub // 2) + FFN_TILES - 2 * KD
def last_width(l, sub): return (KD if sub == 1 else GROUPS[-1][1]) * P
def first_tile0(l, sub): return mix_tile0(l) if sub == 1 else ffn_tile0(l, sub // 2)
def split_by_pool(t):
    for l in range(L):
        for sub in range(3):
            i = t - CONV - last_tile0(l, sub) - KD
            if 0 <= i < KD:
                return i in (1, 3, 6, 7)
            i = t - CONV - first_tile0(l, sub)
            if 0 <= i < HEAD:
                return i < HEAD - 2 and (l, sub) != (0, 0)
    return False
def up_loop(g):
    k0 = 2 if g == 0 else 0
    return k0, (GROUPS[g][1] - k0) // 2 - (g == len(GROUPS) - 1)
def pre_event(l, sub, n): return 6 * l + 2 * sub + n
def post_event(l, sub, n): return 6 * l + 2 * sub + n

TAIL = [("down", 1, 1, 0), ("mean", 1, 0, 0), ("down", 1, 1, 1), ("post", 1, 0, 0), ("down", 1, 1, 2),
        ("post", 1, 0, 2), ("down", 1, 1, 3), ("post", 1, 0, 4), ("down", 1, 1, 4), ("post", 1, 0, 6),
        ("down", 1, 1, 5), ("down", 1, 1, 6), ("mean", 0, 0, 0), ("down", 1, 1, 7),
        ("pre", 0, 0, 0), ("pre", 0, 0, 2), ("pre", 0, 0, 4), ("pre", 0, 0, 6)]
LEAD = ([("mean", 1, 1, 0), ("head", 0, 0, 0), ("post", 1, 1, 0), ("head", 0, 0, 1), ("post", 1, 1, 2),
         ("post", 1, 1, 4), ("post", 1, 1, 6), ("head", 0, 0, 2), ("head", 0, 0, 3), ("mean", 0, 1, 0)]
        + [("pre", 0, 1, k) for k in range(0, KD, 2)])
LEAD_FIRST = ([("square", 0, 0, k) for k in range(0, KD, 2)] + [("split", 0, 0, 0), ("mean", 0, 0, 0)]
              + [(kind, 0, n, k) for k in range(0, KD, 2) for kind, n in (("pre", 0), ("square", 1))]
              + [("head", 0, 0, 0), ("mean", 0, 1, 0), ("head", 0, 0, 1)]
              + [("pre", 0, 1, k) for k in range(0, KD, 2)] + [("head", 0, 0, 2), ("head", 0, 0, 3)])


def tail_steps(l, sub):
    if (l, sub) != (L - 1, 2):
        return TAIL
    return [s for s in TAIL if s[0] != "pre" and s[:2] != ("mean", 0)] + [s for s in LEAD if s[1] == 1]


def lead_steps(l, sub):
    return LEAD_FIRST if (l, sub) == (0, 0) else LEAD


def after(l, sub):
    return (l, sub + 1) if sub < 2 else (l + 1, 0)


def squares_at_down(kind, post, n, k):
    return (0,) if (kind, post, n) == ("mean", 1, 0) else (k,) if kind == "down" and k > 0 else ()


def has_next(cur):
    return cur[0] < L


def norm_orders():
    sq, mean = {}, {}

    def walk(steps, prev, cur):
        for kind, post, n, k in steps:
            if kind == "mean":
                mean[(prev if post else cur) + (post, n)] = len(mean)
            for kk in squares_at_down(kind, post, n, k):
                sq[prev + (1, 1, kk)] = len(sq)
            if kind in ("post", "square") and has_next(cur):
                for kk in (k, k + 1):
                    sq[cur + (0, n, kk)] = len(sq)

    for l in range(L):
        for sub in range(3):
            walk(lead_steps(l, sub), None if (l, sub) == (0, 0) else (l, sub - 1) if sub else (l - 1, 2), (l, sub))
            for k in range(KD):
                sq[l, sub, 1, 0, k] = len(sq)
            walk(tail_steps(l, sub), (l, sub), after(l, sub))
    return sq, mean


SQ_AT, MEAN_AT = norm_orders()

MOD_UNITS = 2 * NMOD
MOD0 = 4
MOD_FREE = 8
def mod_plan(l, j, g, phase):
    plan = {(0, 0): [(0, 0, 2), (0, 1, 2), (1, 0, 4), (1, 1, 2), (2, 0, 3), (2, 2, 1)],
            (0, 1): [(1, 0, 4), (1, 1, 2)],
            (1, 0): [(0, 0, 2), (0, 1, 2), (1, 0, 4), (2, 0, 3), (2, 2, 1)]}.get((l, j), [])
    u = {(0, 0): MOD0, (0, 1): MOD_UNITS, (1, 0): MOD_UNITS + 6}.get((l, j))
    for gg, ph, n in plan:
        if (gg, ph) == (g, phase):
            return u, n
        u += n
    return None
UP, DOWN, UP_LAST = 0, 1, 2

N_FEAT = 22
def attn_items(l):
    lat = [(h, tt) for h in range(HEADS) for tt in range(NTC, NT)]
    return ([(h, tt) for h in range(HEADS) for tt in range(NTC)] if l < L - 1 else []) + lat
def items_before(l): return 0 if l == 0 else len(attn_items(0))
def o_tts(l): return list(range(NT)) if l < L - 1 else list(range(NTC, NT))
def triples(l): return [[0, 1, 2], [3, 4, 5]] if l < L - 1 else [[2, 3], [4, 5]]
OUT_UNITS = MH * 2 * 2


def source_blocks(l, d, j):
    lat = (CTX, SEQ)
    if j < NTC:
        if l == L - 1:
            return None, [lat]
        rest = (P * (j + 1), CTX - P * (j + 1)) if d == 0 else (0, P * j)
        return j, [r for r in (rest, lat) if r[1]]
    rest = (P * (j + 1), T - P * (j + 1)) if d == 0 else (CTX, P * j - CTX)
    return j, [r for r in (rest,) if r[1]]


def sources_of(d, tt):
    if tt < NTC:
        return list(range(0, tt + 1)) if d == 0 else list(range(tt, NTC))
    return list(range(NTC)) + (list(range(NTC, tt + 1)) if d == 0 else list(range(tt, NT)))


def source_slots(l, d):
    out = {}
    for j in range(NT):
        for tt in range(NTC if l == L - 1 else 0, NT):
            if j in sources_of(d, tt):
                out[j, tt] = len(out)
    return out


def product_ranges(l, d, j):
    slots = source_slots(l, d)
    out = []
    for part in (range(NTC), range(NTC, NT)):
        tts = [tt for tt in part if (j, tt) in slots]
        if tts:
            out.append((slots[j, tts[0]], tts[0] * P, len(tts) * P))
    return out


BLOCKS = 2 * NT * MH
def block_index(l, h, j, d): return BLOCKS * l + 2 * NT * h + 2 * j + d
def diag_index(l, h, j, d):
    if l == 0:
        return 2 * NT * h + 2 * j + d
    return BLOCKS + 2 * (NT - NTC) * h + 2 * (j - NTC) + d
def turned_by_dve(l, i):
    return (16 if l else 0) + sum(tt >= NTC for _, tt in attn_items(l)[:i + 1])
def fin_before(l): return 0 if l == 0 else NT * MH
def o_before(l): return NT if l else 0


def hybrid_backbone_kernel(nc, x, c, ctx_in, c_ctx, w_mod, b_mod, norm_pre, norm_post, ffn_w_gate, ffn_w_up,
                           ffn_w_down, w_in, q_norm, w_uq, kv_norm, w_ukv, attn_out_norm, conv_w, conv_b, gate_b,
                           mlstm_norm, w_out, consts, out):
    stack = ExitStack()
    with stack:
        def sb(name, shape, dt=F32, on=stack):
            return on.enter_context(nc.sbuf_tensor(name, shape, dt))

        def overlay(name, shape, dt=F32):
            with nc.sbuf_tensor(name, shape, dt) as t:
                return t

        def sem(name):
            return stack.enter_context(nc.semaphore(name))

        ps = stack.enter_context(nc.psum_tensor("ps", [P, 8, 512], F32))

        xT = sb("xT", [P, KD, T])
        raw = sb("raw", [P, RAW, KD * P])
        wsp = sb("wsp", [P, CONV, 2, KD * P], F32R)
        cst = sb("cst", [P, C_PERS])
        scr = sb("scr", [P, 7, HW])
        modT = sb("modT", [P, NBM, 2])
        modN = sb("modN", [P, NBM, 2])
        vecA = sb("vecA", [P, L, VA_N])
        vecB = sb("vecB", [P, L, VB_N])
        silc = sb("silc", [P, 2, KD])
        gcol = sb("gcol", [P, 3, KD, 2])
        colt = sb("colt", [P, KD, 2])
        kc = sb("kc", [P, 4])
        epsc, onec, zeroc = kc[:, 0:1], kc[:, 1:2], kc[:, 2:3]
        sq2, tmp2, acc, rstd = [scr[:, 0], scr[:, 1]], [scr[:, 2], scr[:, 3]], [scr[:, 4], scr[:, 5]], scr[:, 6]
        sg2, af2 = [scr[:, 0], scr[:, 1]], [scr[:, 2], scr[:, 3]]
        cv = [scr[:, 2 * n:2 * n + 2].rearrange("p a b -> p (a b)") for n in range(2)]
        rstd2 = [scr[:, 2 * n:2 * n + 2].rearrange("p a b -> p (a b)") for n in (1, 2)]
        tmpq = scr[:, 4]
        sqw = cv[0][:, 0:HEADS * VD]
        modL = [modT, modN]
        ident = cst[:, C_ID:C_ID + P]
        ones = cst[:, C_ONES:C_ONES + P]

        with ExitStack() as s:
            hn = sb("hn", [P, 2, KD, T], F32R, s)
            vstage = overlay("vstage", [P, 4, P])
            ostage = overlay("ostage", [P, 2, D])
            with ExitStack() as w:
                sb("vstage_stays", [P, 4, P], F32, w)
                xstage = overlay("xstage", [P, NT, D])
            aT = sb("aT", [P, 2, GMAX, T], F32R, s)
            modw = sb("modw", [P, MODR, 2, 512], F32, s)
            macc = sb("macc", [P, 2, 512], F32, s)
            modw0 = overlay("modw0", [P, MODR0, 2, 512])
            yF = sb("yF", [P, KD, T], F32, s)
        with ExitStack() as s:
            with ExitStack() as w:
                sb("hn_stays", [P, 2, KD, T], F32R, w)
                cosT = sb("cosT", [P, 2, T], F32, w)
                krt = sb("krt", [P, 2, HW], F32, w)
            with ExitStack() as w:
                pblk = sb("pblk", [P, 2, 2, 21, P], F32, w)
                gbc = sb("gbc", [P, 2, T], F32, w)
                dbuf = sb("dbuf", [P, 2, T], F32, w)
                hh = sb("hh", [P, NT, MDH], F32, w)
                ht = sb("ht", [P, 3, MDH], F32, w)
                dn = sb("dn", [P, 2, 4], F32, w)
            qnT = sb("qnT", [P, HEADS, T], F32, s)
            knT = sb("knT", [P, HEADS, T], F32, s)
            va = sb("va", [P, NT, HEADS * VD], F32, s)
            qrT = sb("qrT", [P, 2, T], F32, s)
            pbuf = sb("pbuf", [P, 2, T], F32, s)
            sb("cosT_stays", [P, 2, T], F32, s)
            ptb = sb("ptb", [P, 2, NT, P], F32, s)
            yM = overlay("yM", [P, KD, T])
            rows = overlay("rows", [P, 4, T])
            otok = sb("otok", [P, NT, MW], F32, s)
            cqn = overlay("cqn", [P, 2, 2, T], F32R)
            atok = sb("atok", [P, NT, HEADS * VD], F32, s)
            mixT = overlay("mixT", [P, 2, KD, T], F32R)
            qkT = sb("qkT", [P, KD, T], F32, s)
            vext = sb("vext", [P, NT, MH, MDH + 1], F32, s)
            negG = sb("negG", [P, T], F32, s)
            krT = sb("krT", [P, T], F32, s)
            ckn = sb("ckn", [P, 2, T], F32R, s)
            gb = sb("gb", [P, 2], F32, s)
            colF = sb("colF", [P, NT, GROW], F32, s)
            expnm = sb("expnm", [P, NT, GROW], F32, s)
            stat = sb("stat", [P, 4, 32], F32, s)
            bn6 = sb("bn6", [P, 2, 6], F32, s)
            mv = sb("mv", [P, MH * NT, 2], F32, s)
        krg, ckv, cq = qkT[:, 7], qkT[:, 6], qkT[:, 4:6]
        rI, rX, rT, rB = (rows[0:GROW, n] for n in range(4))

        cst_in, cvec_in, vec_in, x_in, tab_in, gb_in = (sem(n) for n in ("cst_in", "cvec_in", "vec_in", "x_in", "tab_in", "gb_in"))
        raw_in = [sem(f"raw_in{n}") for n in range(RAW)]
        mod_in = [sem(f"mod_in{n}") for n in range(MODR)]
        mod0_in = [sem(f"mod0_in{n}") for n in range(MODR0)]
        mod0_used, mod0_out = sem("mod0_used"), sem("mod0_out")
        whi_done, wlo_done, unit_done = sem("whi_done"), sem("wlo_done"), sem("unit_done")
        silu_done, amul_done, ahi_done, alo_done, yadd_done = (
            sem(n) for n in ("silu_done", "amul_done", "ahi_done", "alo_done", "yadd_done"))
        mod_step, mod_tr, mod_sum = sem("mod_step"), sem("mod_tr"), sem("mod_sum")
        acc_clear, acc_done = sem("acc_clear"), sem("acc_done")
        sq_done, stat_mm, std_done, rstd_done = (sem(n) for n in ("sq_done", "stat_mm", "std_done", "rstd_done"))
        xr_done, hhi_done, hlo_done, yr_done, x_done = (
            sem(n) for n in ("xr_done", "hhi_done", "hlo_done", "yr_done", "x_done"))
        xtr, xev = sem("xtr"), sem("xev")
        vtr, vev = sem("vtr"), sem("vev")
        otr, oev, o_out = sem("otr"), sem("oev"), [sem("o_out0"), sem("o_out1")]
        dchain, achain = sem("dchain"), sem("achain")
        ones_done, gbz_done, pad_done = sem("ones_done"), sem("gbz_done"), sem("pad_done")
        feat_out = sem("feat_out")
        v_out, o_outs, va_out = sem("v_out"), sem("o_outs"), sem("va_out")
        sel_done, gates_out, kro_out = sem("sel_done"), sem("gates_out"), sem("kro_out")
        lsq_done, lstat_done, lstd_done, lat_done = (sem(n) for n in ("lsq_done", "lstat_done", "lstd_done", "lat_done"))
        nabs_done, lnf_done, rows_done, rtr_done, colF_done, expnm_done = (
            sem(n) for n in ("nabs_done", "lnf_done", "rows_done", "rtr_done", "colF_done", "expnm_done"))
        cmid_done, ctap_done, conv_done = sem("cmid_done"), sem("ctap_done"), sem("conv_done")
        sw_done, qr_out = sem("sw_done"), sem("qr_out")
        sc_done, max_done, exp_done, pt_done, pta_out, ptd_out, pv_done, pv_out = (
            sem(n) for n in ("sc_done", "max_done", "exp_done", "pt_done", "pta_out", "ptd_out", "pv_done", "pv_out"))
        g_done, g_out, s_done, dg_done, dx_done, pb_done, mo_done, mo_out = (
            sem(n) for n in ("g_done", "g_out", "s_done", "dg_done", "dx_done", "pb_done", "mo_done", "mo_out"))
        frec_done, afin_done = sem("frec_done"), sem("afin_done")
        atsq_done, fvar_done, fstd_done, fin_done = sem("atsq_done"), sem("fvar_done"), sem("fstd_done"), sem("fin_done")
        mt_done, mhi_done, mlo_done = sem("mt_done"), sem("mhi_done"), sem("mlo_done")

        block = stack.enter_context(nc.Block())

        def y_of(sub):
            return yM if sub == 1 else yF

        def load_rows(eng, i, done):
            l = i // 2
            rows_a = ((0, b_mod[l].rearrange("(r f) -> r f", f=P)),
                      (VA_PRE, norm_pre[l].rearrange("s (r f) -> (s r) f", f=P)),
                      (VA_POST, norm_post[l].rearrange("s (r f) -> (s r) f", f=P)))
            rows_b = ((VB_C, c.rearrange("b (r f) -> (b r) f", f=P)),
                      (VB_CC, c_ctx.rearrange("(r f) -> r f", f=P)),
                      (VB_CW, conv_w[l].rearrange("s (r f) -> (s r) f", f=P)),
                      (VB_CB, conv_b[l].rearrange("(r f) -> r f", f=P)),
                      (VB_QN, q_norm[l].rearrange("(r f) -> r f", f=P)),
                      (VB_KVN, kv_norm[l].rearrange("(r f) -> r f", f=P)),
                      (VB_AN, attn_out_norm[l].rearrange("(r f) -> r f", f=P)),
                      (VB_MN, mlstm_norm[l].rearrange("(r f) -> r f", f=P)))
            for at, v in (rows_a if i % 2 else rows_b):
                eng.dma_start(vstage[at:at + v.shape[0], i], v).then_inc(done, 16)

        @block.sync
        def _(sp):
            def load_tile(t, slot, parts):
                sp.wait_ge(wlo_done, t - RAW + 1 + RAW)
                for dst, src in parts:
                    sp.dma_start(dst, src).then_inc(raw_in[slot], 16)

            def load_mod(u, lm, ul, which):
                w = w_mod[lm].rearrange("(k p) n -> p k n", p=P)
                for j in range(4)[which]:
                    m = 4 * (u - MOD0) + j
                    sp.wait_ge(mod_step, 4 * (m - MODR + 1) + MOD_FREE)
                    sp.dma_start(modw[:, j % MODR], w[:, 2 * j:2 * j + 2, bass.ds(512 * ul, 512)]).then_inc(
                        mod_in[j % MODR], 16)

            def cols_tile(slot, w, at, width=P, k=KD):
                dst = raw[:, slot].rearrange("p (k f) -> p k f", f=P)
                src = w.rearrange("(k p) f -> p k f", p=P)
                h = k // 2
                return [(dst[:, a:b], src[:, a:b, at]) for a, b in ((0, h), (h, k))]

            def ffn(l, j):
                t0 = ffn_tile0(l, j)
                wg, wu, wd = ffn_w_gate[l, j], ffn_w_up[l, j], ffn_w_down[l, j]
                for n in range(2):
                    for b in range(2):
                        for wi, w in enumerate((wg, wu)):
                            load_tile(t0, 2 * b + wi, cols_tile(2 * b + wi, w, slice(b * P, (b + 1) * P)))
                            t0 += 1
                for g, (c0, G) in enumerate(GROUPS):
                    def up_body(i, cols, mod):
                        for b in range(2):
                            for wi, w in enumerate((wg, wu)):
                                s = 2 * b + wi
                                load_tile(t0 + 4 * i + s, s, cols_tile(s, w, cols[b]))
                                if mod is not None:
                                    u = mod[0] + i
                                    load_mod(u, mod[0] // MOD_UNITS, mod[0] % MOD_UNITS + i, slice(s, s + 1))

                    k0, n = up_loop(g)
                    first = c0 + k0
                    mod = mod_plan(l, j, g, UP)
                    if mod is not None and j == 1:
                        sp.wait_ge(unit_done, units_before(ffn_tile0(l, j)))
                    with sp.Fori(0, n) as i:
                        up_body(i, [bass.ds((first + 2 * i + b) * P, P) for b in range(2)], mod)
                    t0 += 4 * n
                    if g == len(GROUPS) - 1:
                        up_body(0, [slice((NCH - 2) * P, (NCH - 1) * P), slice(LAST_F, FF)], mod_plan(l, j, g, UP_LAST))
                        t0 += 4
                    def down_body(i, mod):
                        for s in range(4):
                            cols = bass.ds((4 * i + s) * P, P)
                            if g < len(GROUPS) - 1:
                                parts = cols_tile(s, wd[c0 * P:(c0 + G) * P], cols, k=G)
                            else:
                                parts = [(raw[:, s, 0:(G - 1) * P].rearrange("p (k f) -> p k f", f=P),
                                          wd[c0 * P:(c0 + G - 1) * P].rearrange("(k p) f -> p k f", p=P)[:, :, cols]),
                                         (raw[:, s, (G - 1) * P:G * P], wd[LAST_F:FF, cols])]
                            load_tile(t0 + 4 * i + s, s, parts)
                            if mod is not None:
                                load_mod(mod[0] + i, mod[0] // MOD_UNITS, mod[0] % MOD_UNITS + i, slice(s, s + 1))

                    for n in range(2 if g == len(GROUPS) - 1 else 1):
                        with sp.Fori(0, KD // 4) as i:
                            down_body(i, mod_plan(l, j, g, DOWN))
                        t0 += KD
                assert t0 == ffn_tile0(l, j) + FFN_TILES

            def mixer(l):
                t = mix_tile0(l)
                w = w_in[l]

                def put(parts):
                    nonlocal t
                    load_tile(t, t % RAW, parts)
                    t += 1

                src = w.rearrange("(k p) f -> p k f", p=P)
                for n in range(2):
                    dst = raw[:, t % RAW].rearrange("p (k f) -> p k f", f=P)
                    put([(dst[:, :, 0:ROPE], src[:, :, IN_KR:IN_KR + ROPE]),
                         (dst[:, :, ROPE:P], src[:, :, IN_END - (P - ROPE):IN_END])])
                    for a in (IN_CKV, IN_CQ, IN_CQ + P):
                        put(cols_tile(t % RAW, w, slice(a, a + P)))
                sp.wait_ge(gbz_done, l + 1)
                for n, (r, g) in enumerate(((0, 0), (32, 2), (0, 1), (32, 3))):
                    sp.dma_start(gb[r:r + MH, n // 2:n // 2 + 1], gate_b[l, g].rearrange("(h o) -> h o", o=1)
                                 ).then_inc(gb_in, 16)
                sp.wait_ge(unit_done, units_before(mix_tile0(l)))
                sp.dma_start(cosT[:], consts[:, C_COS:C_COS + 2 * T].rearrange("p (a t) -> p a t", a=2)
                             ).then_inc(tab_in, 16)
                def token_major(a):
                    for q in range(4):
                        dst = raw[:, t % RAW].rearrange("p (k f) -> p k f", f=MW)
                        put([(dst[:, k], w[(2 * q + k) * P:(2 * q + k + 1) * P, a:a + MW]) for k in range(2)])

                token_major(IN_V)
                for n in range(KD):
                    put(cols_tile(t % RAW, w, slice(IN_QK + n * P, IN_QK + (n + 1) * P)))
                token_major(IN_O)
                kv = w_ukv[l].rearrange("p (h c) -> p h c", c=NOPE + VD)
                for a in (0, NOPE):
                    dst = raw[:, t % RAW, 0:HEADS * P].rearrange("p (h f) -> p h f", f=P)
                    put([(dst[:, 2 * b:2 * b + 2], kv[:, 2 * b:2 * b + 2, a:a + P]) for b in range(2)])
                uq = w_uq[l].rearrange("(k p) (h c) -> p k h c", p=P, c=NOPE + ROPE)
                dst = raw[:, t % RAW].rearrange("p (k h f) -> p k h f", k=2, f=NOPE)
                put([(dst[:, k], uq[:, k, :, 0:NOPE]) for k in range(2)])
                dst = raw[:, t % RAW, 0:2 * HEADS * ROPE].rearrange("p (k h f) -> p k h f", k=2, f=ROPE)
                put([(dst[:, k], uq[:, k, :, NOPE:NOPE + ROPE]) for k in range(2)])
                for n in range(2 * KD):
                    put(cols_tile(t % RAW, w_out[l], slice(n % KD * P, (n % KD + 1) * P)))
                assert t == mix_tile0(l) + MIX_TILES

            sp.dma_start(cst[:], consts[:, 0:C_PERS]).then_inc(cst_in, 16)
            w = w_mod[0].rearrange("(k p) n -> p k n", p=P)
            for m in range(4 * MOD0):
                if m == MODR0:
                    for i in range(1, 2 * L):
                        load_rows(sp, i, vec_in)
                if m >= MODR0:
                    sp.wait_ge(mod0_used, m - MODR0 + 1)
                j = m % 4
                sp.dma_start(modw0[:, m % MODR0], w[:, 2 * j:2 * j + 2, m // 4 * 512:(m // 4 + 1) * 512]).then_inc(
                    mod0_in[m % MODR0], 16)
            for l in range(L):
                ffn(l, 0)
                mixer(l)
                ffn(l, 1)
            for n in range(SEQ // P):
                sp.wait_ge(oev, 2 * (n + 1))
                sp.dma_start(out[0, n * P:(n + 1) * P, :], ostage[:, n % 2]).then_inc(o_out[n % 2], 16)
            for n in range(2):
                sp.wait_ge(o_out[n], 16 * (SEQ // P // 2))

        @block.gpsimd
        def _(pool):
            def clear(l, sub, post, n):
                used = MEAN_AT[l, sub, post, 0] + 1 if n == 1 else MEAN_AT[l, sub, post, n] - (1 - post)
                if used > 0:
                    pool.wait_ge(stat_mm, used)
                pool.memset(acc[post], 0.0).then_inc(acc_clear, 1)

            def add(l, sub, post, n, k):
                i = SQ_AT[l, sub, post, n, k]
                w = halves_of(l, sub, post)[n][1]
                pool.wait_ge(sq_done, i + 1)
                if k == 0:
                    pool.wait_ge(acc_clear, 1 + (MEAN_AT[l, sub, post, n]))
                else:
                    pool.wait_ge(acc_done, SQ_AT[l, sub, post, n, k - 1] + 1)
                pool.tensor_tensor(acc[post][:, 0:w], acc[post][:, 0:w], sq2[i % 2][:, 0:w], ALU.add
                                   ).then_inc(acc_done, 1)

            def next_lo(t, width=KD * P):
                if t + CONV < ALL_TILES and split_by_pool(t + 2):
                    cs, slot = t % 2, (t + 2) % RAW
                    pool.wait_ge(whi_done, t + 3)
                    pool.wait_ge(wlo_done, t + 2 + RAW)
                    pool.tensor_tensor(wsp[:, cs, 1, 0:width], raw[:, slot, 0:width],
                                       wsp[:, cs, 0, 0:width].bitcast(F32), ALU.subtract).then_inc(wlo_done, 1)

            def steps(which, prev, cur):
                for kind, post, n, k in which:
                    if kind == "down":
                        next_lo(last_tile0(*prev) + KD + k, last_width(*prev) if k < KD - CONV else KD * P)
                    if kind == "head":
                        next_lo(first_tile0(*cur) + k)
                    if kind == "mean" and n == 0:
                        clear(*(prev if post else cur), post, 1)
                    for kk in squares_at_down(kind, post, n, k):
                        add(*prev, 1, 1, kk)
                    if kind in ("post", "square") and has_next(cur):
                        for kk in (k, k + 1):
                            add(*cur, 0, n, kk)

            for l in range(L):
                for sub in range(3):
                    prev = (l, sub - 1) if sub else (l - 1, 2)
                    if (l, sub) == (0, 0):
                        clear(0, 0, 0, 0)
                    if sub == 1:
                        if l > 0:
                            pool.wait_ge(expnm_done, l)
                        pool.memset(gb[:], 0.0).then_inc(gbz_done, 1)
                    steps(lead_steps(l, sub), prev, (l, sub))
                    if sub == 1:
                        pool.wait_ge(x_done, KD * (post_event(l, 0, 1) + 1))
                        pool.memset(vext[:, :, :, MDH:MDH + 1], 1.0).then_inc(ones_done, 1)
                    pool.wait_ge(yadd_done, last_down0(l, sub) + 1 + 2)
                    clear(l, sub, 1, 0)
                    if after(l, sub)[0] < L:
                        clear(*after(l, sub), 0, 0)
                    for k in range(KD):
                        add(l, sub, 1, 0, k)
                    steps(tail_steps(l, sub), (l, sub), after(l, sub))

        @block.scalar
        def _(act):
            chain = [0]

            def link(ins):
                chain[0] += 1
                ins.then_inc(achain, 1)
                act.wait_ge(achain, chain[0])

            def w_hi(t, slot, cs, nth, used, width=KD * P):
                act.wait_ge(raw_in[slot], 32 * nth)
                if used is not None:
                    act.wait_ge(unit_done, used)
                act.activation(wsp[:, cs, 0, 0:width], raw[:, slot, 0:width], ACT.Copy).then_inc(whi_done, 1)

            def square(l, sub, post, n, k):
                a, w = halves_of(l, sub, post)[n]
                i = SQ_AT[l, sub, post, n, k]
                if post:
                    act.wait_ge(yadd_done, last_down0(l, sub) + KD * n + k + 1 + 2)
                elif (l, sub) == (0, 0):
                    act.wait_ge(xev, KD * (n + 1))
                else:
                    act.wait_ge(x_done, KD * (post_event(l, sub, n) - 2) + k + 1)
                if i >= 2:
                    act.wait_ge(acc_done, i - 1)
                src = y_of(sub) if post else xT
                act.activation(sq2[i % 2][:, 0:w], src[:, k, a:a + w], ACT.Square).then_inc(sq_done, 1)

            def root(l, sub, post, n):
                w = halves_of(l, sub, post)[n][1]
                e = MEAN_AT[l, sub, post, n]
                act.wait_ge(stat_mm, e + 1)
                bank = ps[:, 6 + e % 2, 0:w]
                act.activation(bank, bank, ACT.Sqrt, bias=epsc).then_inc(std_done, 1)

            def high(l, sub, n, k):
                a, w = halves_of(l, sub, 0)[n]
                act.wait_ge(xr_done, KD * pre_event(l, sub, n) + k + 1)
                for s, sw, v in segments(a, w):
                    ins = act.activation(hn[:, 0, k, s:s + sw], tmp2[k % 2][:, s - a:s - a + sw], ACT.Identity,
                                         bias=gcol[:, 1, k, v:v + 1])
                ins.then_inc(hhi_done, 1)

            def next_hi(t, width=KD * P):
                if t + CONV < ALL_TILES:
                    w_hi(t + 2, (t + 2) % RAW, t % 2, (t + 2) // RAW + 1, units_before(t + 1), width)

            def steps(which, prev, cur):
                for kind, post, n, k in which:
                    if kind == "down":
                        t = last_tile0(*prev) + KD + k
                        next_hi(t, last_width(*prev) if k < KD - CONV else KD * P)
                    if kind == "head":
                        next_hi(first_tile0(*cur) + k)
                    if kind == "split":
                        for t in range(CONV):
                            w_hi(t, t, t, 1, None)
                    if kind == "mean":
                        root(*(prev if post else cur), post, n)
                    for kk in squares_at_down(kind, post, n, k):
                        square(*prev, 1, 1, kk)
                    if kind in ("post", "square") and has_next(cur):
                        for kk in (k, k + 1):
                            square(*cur, 0, n, kk)
                    if kind == "pre":
                        for kk in (k, k + 1):
                            high(*cur, n, kk)

            def last_pass(l, sub):
                t0 = last_tile0(l, sub)
                d0, i0 = last_down0(l, sub), SQ_AT[l, sub, 1, 0, 0]
                a, w = halves_of(l, sub, 1)[0]
                y = y_of(sub)
                with act.Fori(0, KD // 4) as i:
                    for s in range(4):
                        act.wait_ge(yadd_done, d0 + 4 * i + s + 1 + 2)
                        act.wait_ge(acc_done, i0 + 4 * i + s - 1)
                        act.activation(sq2[(i0 + s) % 2][:, 0:w], y[:, 4 * i + s, a:a + w], ACT.Square
                                       ).then_inc(sq_done, 1)
                        w_hi(t0 + 4 * i + s + 2, (s + 2) % RAW, s % 2, (t0 + s + 2) // RAW + 1 + i,
                             units_before(t0) + 4 * i + s + 1, last_width(l, sub))

            def ffn(l, j):
                t0, q0 = ffn_tile0(l, j), ffn_pair0(l, j)
                hv = halves_of(l, 2 * j, 1)
                for n, (a, w) in enumerate(hv):
                    for b in range(2):
                        t, q = t0 + HEAD * n + 2 * b, q0 + 2 * n + b
                        act.wait_ge(unit_done, units_before(t) + 1)
                        act.wait_ge(acc_done, SQ_AT[l, 2 * j, 0, 1, KD - 1] + 1)
                        act.wait_ge(amul_done, q + 1)
                        act.activation(sg2[b][:, 0:w], ps[:, HEAD_BANKS[n][2 * b], 0:w], ACT.Silu
                                       ).then_inc(silu_done, 1)
                        if n == 1:
                            next_hi(t)
                        act.wait_ge(amul_done, q + 3)
                        act.activation(aT[:, 0, b, a:a + w], af2[b][:, 0:w], ACT.Copy).then_inc(ahi_done, 1)
                        if n == 1:
                            next_hi(t + 1)
                t0 += 2 * HEAD
                q0 += HEAD
                for g, (c0, G) in enumerate(GROUPS):
                    def up_body(i, k0, last):
                        for b in range(2):
                            t = t0 + 4 * i + 2 * b
                            q = q0 + 4 * i + 2 * b
                            used = units_before(t0) + 8 * i + 4 * b
                            s = 2 * b
                            for n, (a, w) in enumerate(hv):
                                act.wait_ge(unit_done, used + n + 1)
                                act.wait_ge(amul_done, q + n + 1)
                                act.activation(sg2[n][:, 0:w], ps[:, n, 0:w], ACT.Silu).then_inc(silu_done, 1)
                            w_hi(t + 2, (s + 2) % RAW, 0, (t0 + 2 * b + 2) // RAW + 1 + i, used + 2)
                            kc = k0 + 2 * i + b
                            for n, (a, w) in enumerate(hv):
                                act.wait_ge(amul_done, q + n + 3)
                                lo = OVER if last and b == 1 else 0
                                act.activation(aT[lo:P, 0, kc, a:a + w], af2[n][lo:P, 0:w], ACT.Copy
                                               ).then_inc(ahi_done, 1)
                            w_hi(t + 3, (s + 3) % RAW, 1, (t0 + 2 * b + 3) // RAW + 1 + i, used + 4)

                    k0, n_loop = up_loop(g)
                    with act.Fori(0, n_loop) as i:
                        up_body(i, k0, False)
                    if g == len(GROUPS) - 1:
                        up_body(n_loop, k0, True)
                        return
                    t0 += 2 * (G - k0)
                    q0 += 2 * (G - k0)
                    with act.Fori(0, KD // 4) as i:
                        for s in range(4):
                            w_hi(t0 + 4 * i + s + 2, (s + 2) % RAW, s % 2, (t0 + s + 2) // RAW + 1 + i,
                                 units_before(t0) + 8 * i + 2 * s + 2)
                    t0 += KD

            def mixer(l):
                t0 = mix_tile0(l)
                fb = 2 * N_FEAT * l

                def hi_after(i):
                    next_hi(t0 + i)

                def evac(f, dst, halves, ns=(0, 1)):
                    for n in ns:
                        a, w = halves[n]
                        act.wait_ge(unit_done, feat_unit(l, f, n))
                        act.activation(dst[:, a:a + w], ps[:, feat_bank(f, n), 0:w], ACT.Copy).then_inc(feat_out, 1)

                fh, oh = full_halves(l), out_halves(l)
                low = (krg, ckv, cq[:, 0], cq[:, 1])
                act.wait_ge(yr_done, KD * (post_event(l, 0, 1) + 1))
                for f in range(HEAD):
                    evac(f, low[f], fh, (0,))
                for f in range(2):
                    evac(f, low[f], fh, (1,))
                    hi_after(HEAD + f)
                act.wait_ge(gb_in, 64 * (l + 1))
                for z, dst in enumerate((rI, rX)):
                    for n, (a, w) in enumerate(fh):
                        act.wait_ge(sel_done, 8 * l + 2 * z + n + 1)
                        act.activation(dst[:, a:a + w], ps[0:GROW, 6 + n, 0:w], ACT.Identity,
                                       bias=gb[0:GROW, z:z + 1]).then_inc(gates_out, 1)
                    evac(2 + z, low[2 + z], fh, (1,))
                    hi_after(HEAD + 2 + z)
                for i, (src, halves) in enumerate(((ckv, fh), (cq[:, 0], oh), (cq[:, 1], oh))):
                    for n, (a, w) in enumerate(halves):
                        if i == 2:
                            act.wait_ge(lstat_done, 6 * l + 3 + n)
                        if i == 1:
                            act.wait_ge(lstat_done, 6 * l + 1 + n)
                        act.wait_ge(feat_out, fb + 2 * HEAD)
                        act.activation(sq2[n][:, 0:w], src[:, a:a + w], ACT.Square).then_inc(lsq_done, 1)
                    if i != 1:
                        for n, (a, w) in enumerate(halves):
                            act.wait_ge(lstat_done, 6 * l + 2 * i + n + 1)
                            act.activation(rstd2[i // 2][:, a:a + w], ps[:, 6 + n, 0:w], ACT.Sqrt, bias=epsc,
                                           scale=float(D // (KVL if i == 0 else QL))).then_inc(lstd_done, 1)
                hi_after(V_TILE)
                act.wait_ge(nabs_done, l + 1)
                link(act.activation(rT, rT, ACT.Exp))
                act.activation(rT, rT, ACT.Ln, bias=onec[0:GROW]).then_inc(lnf_done, 1)
                for i in range(V_TILE + 1, QK_TILE):
                    hi_after(i)
                for n in range(KD):
                    f = 4 + n
                    halves = oh if n < MH else fh
                    if n == 1:
                        act.wait_ge(lat_done, 6 * (l + 1))
                    u = qkT[:, n]
                    evac(f, u, halves)
                    hi_after(QK_TILE + n)
                    act.wait_ge(feat_out, fb + 2 * f + 2)
                    lo = halves[0][0]
                    act.activation(cv[n % 2][:, lo:T], u[:, lo:T], ACT.Identity, bias=vecB[:, l, VB_CB + n:VB_CB + n + 1],
                                   scale=vecB[:, l, VB_CW + KD + n:VB_CW + KD + n + 1]).then_inc(cmid_done, 1)
                    if n >= 1:
                        silu_conv(l, n - 1)
                silu_conv(l, KD - 1)
                act.wait_ge(rtr_done, 2 * (l + 1))
                act.activation(expnm[:].rearrange("p a b -> p (a b)"), ps[:, 7, 0:NT * GROW], ACT.Exp
                               ).then_inc(expnm_done, 1)
                for i in range(O_TILE, UKN_TILE):
                    hi_after(i)
                for i, tt in enumerate(o_tts(l)):
                    act.wait_ge(unit_done, unit_of(l, UKN_TILE - 1, i))
                    if i == 0:
                        act.wait_ge(colF_done, l + 1)
                    act.activation(otok[:, tt], ps[:, tt], ACT.Sigmoid).then_inc(o_outs, 1)
                for h in range(HEADS):
                    evac(12 + h, knT[:, h], fh)
                hi_after(UKN_TILE)
                for tt in range(NT):
                    act.wait_ge(unit_done, unit_of(l, UVA_TILE, tt))
                    act.activation(va[:, tt], ps[:, tt], ACT.Copy).then_inc(va_out, 1)
                hi_after(UVA_TILE)
                for h in range(HEADS):
                    evac(16 + h, qnT[:, h], oh)
                hi_after(UQN_TILE)
                for z in range(2):
                    evac(20 + z, cv[z], oh)
                hi_after(UQR_TILE)
                items = attn_items(l)
                a0 = items_before(l)

                def attn_exp(i):
                    h, tt = items[i]
                    nk = T if tt >= NTC else CTX
                    act.wait_ge(max_done, a0 + i + 1)
                    if i >= 2:
                        act.wait_ge(pt_done, a0 + i - 1)
                    b = 2 * (i % 2)
                    src = ps[:, b:b + 2, 0:HW] if nk == T else ps[:, b, 0:CTX]
                    dst = pbuf[:, i % 2, 0:nk]
                    if nk == T:
                        dst = dst.rearrange("p (a b) -> p a b", a=2)
                    act.activation(dst, src, ACT.Exp, bias=stat[:, 0, i % 8:i % 8 + 1], scale=SM_SCALE,
                                   accum_out=stat[:, 1, i % 8:i % 8 + 1]).then_inc(exp_done, 1)

                def pt_evac(i):
                    h, tt = items[i]
                    act.wait_ge(pt_done, a0 + i + 1)
                    if i >= 2:
                        act.wait_ge(pv_done, a0 + i - 1)
                    ns = 4 if tt >= NTC else NTC
                    act.activation(ptb[:, i % 2, 0:ns].rearrange("p a b -> p (a b)"), ps[:, 4, 0:ns * P], ACT.Copy
                                   ).then_inc(pta_out, 1)

                for i in range(len(items) + 1):
                    if i < len(items):
                        attn_exp(i)
                    if i >= 1:
                        pt_evac(i - 1)
                for h in range(MH):
                    for d in range(2):
                        for z, (a, w) in enumerate(((0, CTX), (CTX, SEQ))):
                            gi = 4 * (MH * l + h) + 2 * d + z
                            act.wait_ge(g_done, gi + 1)
                            if h > 0:
                                act.wait_ge(dg_done, diag_index(l, h - 1, NT - 1, 1) + 1)
                            act.activation(gbc[:, d, a:a + w], ps[:, z, 0:w], ACT.Copy).then_inc(g_out, 1)
                    for j in range(NT):
                        for d in range(2):
                            diag, rest = source_blocks(l, d, j)
                            col = colF[:, j, 32 * d + h:32 * d + h + 1]
                            i = block_index(l, h, j, d)
                            if i >= 2:
                                act.wait_ge(pb_done, i - 1)
                            act.wait_ge(g_out, 4 * (MH * l + h) + 2 * d + 2)
                            ins = None
                            for a, w in rest:
                                ins = act.activation(dbuf[:, d, a:a + w], gbc[:, d, a:a + w], ACT.Exp, bias=col)
                            if diag is not None:
                                act.wait_ge(dg_done, diag_index(l, h, j, d) + 1)
                                ins = act.activation(dbuf[:, d, diag * P:(diag + 1) * P],
                                                     dbuf[:, d, diag * P:(diag + 1) * P], ACT.Exp)
                            ins.then_inc(dx_done, 1)
                act.wait_ge(pv_out, a0 + len(items))
                t1 = o_tts(l)[0]
                for tt in o_tts(l):
                    if tt > t1:
                        act.wait_ge(atsq_done, (tt - t1) + (NT if l else 0))
                    act.activation(sqw, atok[:, tt], ACT.Square, accum_out=stat[:, 3, tt:tt + 1]).then_inc(atsq_done, 1)
                for last in range(2):
                    if last:
                        act.wait_ge(frec_done, l + 1)
                        for tt in o_tts(l):
                            act.activation(atok[:, tt], atok[:, tt], ACT.Identity, scale=stat[:, 3, tt:tt + 1],
                                           bias=zeroc).then_inc(afin_done, 1)
                    act.wait_ge(fvar_done, 2 * l + last + 1)
                    var = stat[:, 2, 0:NT * MH].rearrange("p (h t) -> p h t", h=MH)
                    var = var[:, MH - 1:MH, t1:NT] if last else var[:, 0:MH - 1, t1:NT]
                    act.activation(var, var, ACT.Sqrt, bias=epsc).then_inc(fstd_done, 1)
                    if not last:
                        act.wait_ge(atsq_done, (NT - t1) + (NT if l else 0))
                        act.activation(stat[:, 3, t1:NT], stat[:, 3, t1:NT], ACT.Sqrt, bias=epsc,
                                       scale=1.0 / (HEADS * VD)).then_inc(fstd_done, 1)
                for n, (a, w) in enumerate(oh):
                    for cidx in range(KD):
                        i = 16 * l + KD * n + cidx
                        act.wait_ge(mt_done, i + 1)
                        act.activation(mixT[:, 0, cidx, a:a + w], ps[:, i % 4, 0:w], ACT.Identity,
                                       scale=vecB[:, l, VB_AN + cidx:VB_AN + cidx + 1], bias=zeroc).then_inc(mhi_done, 1)

            def silu_conv(l, n):
                lo = (out_halves(l) if n < MH else full_halves(l))[0][0]
                act.wait_ge(ctap_done, KD * l + n + 1)
                act.activation(qkT[:, n, lo:T], cv[n % 2][:, lo:T], ACT.Silu).then_inc(conv_done, 1)

            load_rows(act, 0, cvec_in)
            act.dma_start(xstage[:, 0:NTC], ctx_in[0].rearrange("(t p) d -> p t d", p=P)).then_inc(x_in, 16)
            act.dma_start(xstage[:, NTC:NT], x[0].rearrange("(t p) d -> p t d", p=P)).then_inc(x_in, 16)
            act.wait_ge(vev, 1)
            act.activation(silc[:, 0], vecB[:, 0, VB_C:VB_C + KD], ACT.Silu).then_inc(silu_done, 1)
            act.activation(silc[:, 1], vecB[:, 0, VB_CC:VB_CC + KD], ACT.Silu).then_inc(silu_done, 1)
            for u in range(MOD0):
                act.wait_ge(mod0_used, 4 * (u + 1))
                if u >= 2:
                    act.wait_ge(mod_tr, u - 1)
                act.activation(macc[0:2, u % 2], ps[0:2, u % 2], ACT.Copy).then_inc(mod0_out, 1)
            for l in range(L):
                for sub in range(3):
                    steps(lead_steps(l, sub), (l, sub - 1) if sub else (l - 1, 2), (l, sub))
                    if sub == 1:
                        mixer(l)
                    else:
                        ffn(l, sub // 2)
                    last_pass(l, sub)
                    steps(tail_steps(l, sub), (l, sub), after(l, sub))
            for i in range(2 * (SEQ // P)):
                act.wait_ge(otr, i + 1)
                if i >= 4:
                    act.wait_ge(o_out[(i // 2) % 2], 16 * (i // 4))
                act.activation(ostage[:, (i // 2) % 2, (i % 2) * 512:(i % 2 + 1) * 512], ps[:, i % 4], ACT.Copy
                               ).then_inc(oev, 1)

        @block.vector
        def _(dve):
            chain = [0]

            def link(ins):
                chain[0] += 1
                ins.then_inc(dchain, 1)
                dve.wait_ge(dchain, chain[0])

            def w_lo(t, slot, cs, width=KD * P):
                dve.wait_ge(whi_done, t + 1)
                dve.tensor_tensor(wsp[:, cs, 1, 0:width], raw[:, slot, 0:width], wsp[:, cs, 0, 0:width].bitcast(F32),
                                  ALU.subtract).then_inc(wlo_done, 1)

            def next_lo(t, width=KD * P):
                if t + CONV < ALL_TILES and not split_by_pool(t + 2):
                    if split_by_pool(t + 1):
                        dve.wait_ge(wlo_done, t + 2 + RAW)
                    w_lo(t + 2, (t + 2) % RAW, t % 2, width)

            def mod_tiles(u, js):
                for j in js:
                    m = 4 * (u - MOD0) + j
                    nth = 2 * (u - MOD0) + j // 2 + 1
                    dve.wait_ge(mod_in[j % MODR], 16 * nth)
                    for kk in range(2):
                        k = 2 * j + kk
                        w = modw[:, j % MODR, kk]
                        for v in range(2):
                            s = 16 * (u - MOD0) + 2 * k + v + MOD_FREE
                            if k == 0:
                                dve.wait_ge(mod_tr, u)
                                ins = dve.tensor_scalar(macc[:, v], w, silc[:, v, k:k + 1], None, ALU.mult)
                            else:
                                dve.wait_ge(mod_step, s - 1)
                                ins = dve.scalar_tensor_tensor(out=macc[:, v], in0=w, scalar=silc[:, v, k:k + 1],
                                                               in1=macc[:, v], op0=ALU.mult, op1=ALU.add)
                            ins.then_inc(mod_step, 1)

            def mod_reduce(u, lm, ul):
                dve.wait_ge(mod_tr, u + 1)
                for v in range(2):
                    ins = dve.tensor_reduce(modL[lm][:, bass.ds(4 * ul, 4), v],
                                            ps[:, 6 + v].rearrange("p (a b) -> p a b", a=4), AX.X, ALU.add)
                ins.then_inc(mod_sum, 1)

            def columns(l, sub, i):
                m, b = modL[l], vecA[:, l]
                part = (1, 0, 2)[i]
                dve.wait_ge(mod_sum, l * MOD_UNITS + 6 * sub + 2 * (part + 1))
                if i < 2 and (l, sub) != (0, 0):
                    dve.wait_ge(hlo_done, KD * pre_event(l, sub, 0))
                if i == 2 and (l, sub) != (0, 0):
                    dve.wait_ge(x_done, KD * post_event(l, sub, 0))
                r = slice((3 * sub + part) * KD, (3 * sub + part + 1) * KD)
                if part == 0:
                    link(dve.tensor_tensor(gcol[:, 1], m[:, r], b[:, r].unsqueeze(2).broadcast_to([P, KD, 2]), ALU.add))
                    return
                link(dve.tensor_tensor(colt[:], m[:, r], b[:, r].unsqueeze(2).broadcast_to([P, KD, 2]), ALU.add))
                gain = b[:, (VA_PRE if part == 1 else VA_POST) + sub * KD:][:, 0:KD].unsqueeze(2).broadcast_to([P, KD, 2])
                link(dve.scalar_tensor_tensor(out=gcol[:, i], in0=colt[:],
                                              scalar=1.0 if part == 1 else 1.0 if sub == 1 else 0.5, in1=gain,
                                              op0=ALU.add if part == 1 else ALU.mult, op1=ALU.mult))

            def inv_root(l, sub, post, n):
                w = halves_of(l, sub, post)[n][1]
                e = MEAN_AT[l, sub, post, n]
                dve.wait_ge(std_done, e + 1)
                if post:
                    dve.wait_ge(xr_done, KD * (pre_event(l, sub, 1) + 1))
                elif (l, sub) != (0, 0):
                    dve.wait_ge(yr_done, KD * (post_event(l, sub, n) - 1))
                if n == 1 and post and has_next(after(l, sub)):
                    dve.wait_ge(xr_done, KD * (pre_event(*after(l, sub), 0) + 1))
                if n == 1 and (post or (l, sub) == (0, 0)):
                    dve.wait_ge(yr_done if post else xr_done, KD * (pre_event(l, sub, 0) + 1))
                dve.reciprocal(rstd[:, 0:w], ps[:, 6 + e % 2, 0:w]).then_inc(rstd_done, 1)
                dve.wait_ge(rstd_done, e + 1)

            def pre(l, sub, n, k):
                a, w = halves_of(l, sub, 0)[n]
                p = pre_event(l, sub, n)
                if k == 0:
                    if (l, sub) != (0, 0):
                        prev = (l, sub - 1) if sub else (l - 1, 2)
                        dve.wait_ge(unit_done, units_before(last_tile0(*prev)) + 1)
                        dve.wait_ge(x_done, KD * (post_event(*prev, n) + 1))
                    if n == 1:
                        dve.wait_ge(hlo_done, KD * p)
                for kk in (k, k + 1):
                    if kk >= 2:
                        dve.wait_ge(hlo_done, KD * p + kk - 1)
                    for s, sw, v in segments(a, w):
                        ins = dve.scalar_tensor_tensor(out=tmp2[kk % 2][:, s - a:s - a + sw], in0=xT[:, kk, s:s + sw],
                                                       scalar=gcol[:, 0, kk, v:v + 1], in1=rstd[:, s - a:s - a + sw],
                                                       op0=ALU.mult, op1=ALU.mult)
                    ins.then_inc(xr_done, 1)
                for kk in (k, k + 1):
                    dve.wait_ge(hhi_done, KD * p + kk + 1)
                    for s, sw, v in segments(a, w):
                        ins = dve.scalar_tensor_tensor(out=hn[:, 1, kk, s:s + sw], in0=tmp2[kk % 2][:, s - a:s - a + sw],
                                                       scalar=gcol[:, 1, kk, v:v + 1],
                                                       in1=hn[:, 0, kk, s:s + sw].bitcast(F32),
                                                       op0=ALU.add, op1=ALU.subtract)
                    ins.then_inc(hlo_done, 1)
            def post_norm(l, sub, n, k):
                a, w = halves_of(l, sub, 1)[n]
                y = y_of(sub)
                r = post_event(l, sub, n)
                if k == 0:
                    dve.wait_ge(hlo_done, KD * (pre_event(l, sub, 1) + 1 + (n if has_next(after(l, sub)) else 0)))
                    if r > 0:
                        dve.wait_ge(x_done, KD * r)
                for kk in (k, k + 1):
                    if kk >= 2:
                        dve.wait_ge(x_done, KD * r + kk - 1)
                    dve.tensor_tensor(tmp2[kk % 2][:, 0:w], y[:, kk, a:a + w], rstd[:, 0:w], ALU.mult
                                      ).then_inc(yr_done, 1)
                for kk in (k, k + 1):
                    dve.wait_ge(yr_done, KD * r + kk + 1)
                    for s, sw, v in segments(a, w):
                        ins = dve.scalar_tensor_tensor(out=xT[:, kk, s:s + sw], in0=tmp2[kk % 2][:, s - a:s - a + sw],
                                                       scalar=gcol[:, 2, kk, v:v + 1], in1=xT[:, kk, s:s + sw],
                                                       op0=ALU.mult, op1=ALU.add)
                    ins.then_inc(x_done, 1)

            def down_evac(unit, dt, hv, n, before):
                a, w = hv[n]
                dve.wait_ge(unit_done, unit)
                dst = yF[:, dt, a:a + w]
                src = ps[:, 4 + n, 0:w]
                if before is None:
                    dve.tensor_copy(dst, src).then_inc(yadd_done, 1)
                else:
                    dve.wait_ge(yadd_done, before)
                    dve.tensor_tensor(dst, src, dst, ALU.add).then_inc(yadd_done, 1)

            def steps(which, prev, cur):
                for kind, post, n, k in which:
                    if kind == "down":
                        t = last_tile0(*prev) + KD + k
                        last_evac(*prev, 1, k, 4 + k % 2)
                        next_lo(t, last_width(*prev) if k < KD - CONV else KD * P)
                    if kind == "head":
                        next_lo(first_tile0(*cur) + k)
                    if kind == "split":
                        for t in range(CONV):
                            w_lo(t, t, t)
                    if kind == "mean":
                        inv_root(*(prev if post else cur), post, n)
                    if kind == "post":
                        post_norm(*prev, n, k)
                    if kind == "pre":
                        pre(*cur, n, k)

            def last_evac(l, sub, n, dt, bank):
                a, w = halves_of(l, sub, 1)[n]
                dst = y_of(sub)[:, dt, a:a + w]
                src = ps[:, bank, 0:w]
                dve.wait_ge(unit_done, units_before(last_tile0(l, sub)) + KD * n + dt + 1)
                if sub == 1:
                    dve.tensor_copy(dst, src).then_inc(yadd_done, 1)
                else:
                    dve.wait_ge(yadd_done, last_down0(l, sub) + 2)
                    dve.tensor_tensor(dst, src, dst, ALU.add).then_inc(yadd_done, 1)

            def last_pass(l, sub):
                t0 = last_tile0(l, sub)
                with dve.Fori(0, KD // 4) as i:
                    for s in range(4):
                        last_evac(l, sub, 0, 4 * i + s, 4 + s % 2)
                        w_lo(t0 + 4 * i + s + 2, (s + 2) % RAW, s % 2, last_width(l, sub))

            def ffn(l, j):
                t0, q0, d0 = ffn_tile0(l, j), ffn_pair0(l, j), ffn_down0(l, j)
                hv = halves_of(l, 2 * j, 1)
                def activated(q, b, kc, a, w, bank, up, lo=0):
                    dve.wait_ge(unit_done, up)
                    dve.wait_ge(silu_done, q + 3)
                    dve.wait_ge(alo_done, q + 1)
                    dve.tensor_tensor(af2[b][:, 0:w], ps[:, bank, 0:w], sg2[b][:, 0:w], ALU.mult
                                      ).then_inc(amul_done, 1)
                    dve.wait_ge(ahi_done, q + 1)
                    dve.tensor_tensor(aT[lo:P, 1, kc, a:a + w], af2[b][lo:P, 0:w],
                                      aT[lo:P, 0, kc, a:a + w].bitcast(F32), ALU.subtract).then_inc(alo_done, 1)

                dve.wait_ge(hlo_done, KD * (pre_event(l, 2 * j, 1) + 1))
                for n, (a, w) in enumerate(hv):
                    for b in range(2):
                        t = t0 + HEAD * n + 2 * b
                        if n == 1:
                            next_lo(t)
                        activated(q0 + 2 * n + b, b, b, a, w, HEAD_BANKS[n][2 * b + 1], units_before(t) + 2)
                        if n == 1:
                            next_lo(t + 1)
                t0 += 2 * HEAD
                q0 += HEAD
                for g, (c0, G) in enumerate(GROUPS):
                    def up_body(i, k0, last, mod):
                        for b in range(2):
                            t = t0 + 4 * i + 2 * b
                            q = q0 + 4 * i + 2 * b
                            s = 2 * b
                            used = units_before(t0) + 8 * i + 4 * b + 2
                            if mod is not None:
                                mod_tiles(mod[0] + i, (2 * b, 2 * b + 1))
                            w_lo(t + 2, (s + 2) % RAW, 0)
                            for n, (a, w) in enumerate(hv):
                                activated(q + n, n, k0 + 2 * i + b, a, w, 2 + n, used + n + 1,
                                          OVER if last and b == 1 else 0)
                            w_lo(t + 3, (s + 3) % RAW, 1)
                        if mod is not None:
                            mod_reduce(mod[0] + i, mod[0] // MOD_UNITS, mod[0] % MOD_UNITS + i)

                    if g == len(GROUPS) - 1:
                        dve.wait_ge(unit_done, units_before(t0))
                        for half in range(2):
                            ins = dve.memset(aT[0:OVER, half, G - 1].bitcast(F32), 0.0)
                        ins.then_inc(pad_done, 1)
                    k0, n_loop = up_loop(g)
                    mod = mod_plan(l, j, g, UP)
                    with dve.Fori(0, n_loop) as i:
                        up_body(i, k0, False, mod)
                    if g == len(GROUPS) - 1:
                        last_mod = mod_plan(l, j, g, UP_LAST)
                        up_body(n_loop, k0, True, last_mod and (last_mod[0] - n_loop, 1))
                        return
                    t0 += 2 * (G - k0)
                    q0 += 2 * (G - k0)
                    mod = mod_plan(l, j, g, DOWN)
                    with dve.Fori(0, KD // 4) as i:
                        for s in range(4):
                            t, d = t0 + 4 * i + s, d0 + 8 * i + 2 * s
                            unit = units_before(t0) + 8 * i + 2 * s + 1
                            down_evac(unit, 4 * i + s, hv, 0, None if g == 0 else d - DOWN_OUT + 3)
                            if mod is not None:
                                mod_tiles(mod[0] + i, (s,))
                            down_evac(unit + 1, 4 * i + s, hv, 1, None if g == 0 else d - DOWN_OUT + 4)
                            w_lo(t + 2, (s + 2) % RAW, s % 2)
                        if mod is not None:
                            mod_reduce(mod[0] + i, mod[0] // MOD_UNITS, mod[0] % MOD_UNITS + i)
                    t0 += KD
                    d0 += DOWN_OUT

            def mixer(l):
                t0 = mix_tile0(l)
                fb = 2 * N_FEAT * l
                fh, oh = full_halves(l), out_halves(l)

                def lo_after(i):
                    next_lo(t0 + i)

                for i in range(HEAD, 2 * HEAD):
                    lo_after(i)
                dve.wait_ge(tab_in, 16 * (l + 1))
                for n, (a, w) in enumerate(fh):
                    dve.wait_ge(sel_done, 8 * l + 4 + n + 1)
                    dve.tensor_tensor(krT[:, a:a + w], ps[:, 6 + n, 0:w], cosT[:, 0, a:a + w], ALU.mult
                                      ).then_inc(kro_out, 1)
                for n, (a, w) in enumerate(fh):
                    dve.wait_ge(sel_done, 8 * l + 6 + n + 1)
                    link(dve.tensor_tensor(krt[:, n, 0:w], ps[:, 6 + n, 0:w], cosT[:, 1, a:a + w], ALU.mult))
                    dve.tensor_tensor(krT[:, a:a + w], krT[:, a:a + w], krt[:, n, 0:w], ALU.add
                                      ).then_inc(kro_out, 1)
                dve.wait_ge(gates_out, 4 * (l + 1))
                dve.scalar_tensor_tensor(out=rT, in0=rX, scalar=-1.0, in1=rX, op0=ALU.mult, op1=ALU.min
                                         ).then_inc(nabs_done, 1)
                for i, (src, dst, r2, gain, halves) in enumerate((
                        (ckv, ckn, 0, VB_KVN, fh), (cq[:, 0], cqn[:, :, 0], 1, VB_QN, oh),
                        (cq[:, 1], cqn[:, :, 1], 1, VB_QN + 1, oh))):
                    for n, (a, w) in enumerate(halves):
                        if i < 2:
                            dve.wait_ge(lstd_done, 4 * l + 2 * i + n + 1)
                            link(dve.reciprocal(rstd2[r2][:, a:a + w], rstd2[r2][:, a:a + w]))
                        v = src[:, a:a + w]
                        link(dve.scalar_tensor_tensor(out=v, in0=v, scalar=vecB[:, l, gain:gain + 1],
                                                      in1=rstd2[r2][:, a:a + w], op0=ALU.mult, op1=ALU.mult))
                        link(dve.tensor_copy(dst[:, 0, a:a + w], v))
                        dve.tensor_tensor(dst[:, 1, a:a + w], v, dst[:, 0, a:a + w].bitcast(F32), ALU.subtract
                                          ).then_inc(lat_done, 1)
                    lo_after(V_TILE + i)
                lo_after(QK_TILE - 1)
                for tt in range(NT):
                    dve.wait_ge(unit_done, unit_of(l, QK_TILE - 1, tt))
                    dve.tensor_copy(vext[:, tt, :, 0:MDH], ps[:, tt].rearrange("p (h e) -> p h e", h=MH)
                                    ).then_inc(v_out, 1)
                dve.wait_ge(lnf_done, l + 1)
                link(dve.scalar_tensor_tensor(out=rT, in0=rX, scalar=0.0, in1=rT, op0=ALU.min, op1=ALU.subtract))

                def scans(dst, src, op, post_op):
                    link(dve.tensor_tensor_scan(dst[0:32], src[0:32], src[0:32], 0.0, op, post_op))
                    back = slice(None, None, -1)
                    link(dve.tensor_tensor_scan(dst[32:GROW, 0:CTX][:, back], src[32:GROW, 0:CTX][:, back],
                                                src[32:GROW, 0:CTX][:, back], 0.0, op, post_op))
                    link(dve.tensor_tensor_scan(dst[32:GROW, CTX:T][:, back], src[32:GROW, CTX:T][:, back],
                                                src[32:GROW, CTX:T][:, back], dst[32:GROW, 0:1], op, post_op))

                scans(rB, rT, ALU.add, ALU.bypass)
                link(dve.tensor_tensor(rI, rI, rB, ALU.subtract))
                scans(rX, rI, ALU.max, ALU.max)
                link(dve.scalar_tensor_tensor(out=rB, in0=rB, scalar=-1.0, in1=rX, op0=ALU.mult, op1=ALU.subtract))
                dve.tensor_scalar(negG[0:GROW], rX, -1.0, None, ALU.mult).then_inc(rows_done, 1)
                for n in range(KD):
                    dve.wait_ge(cmid_done, KD * l + n + 1)
                    u, out_, wt = qkT[:, n], cv[n % 2], vecB[:, l]
                    streams = ((0, CTX), (CTX, SEQ)) if l < L - 1 or n >= MH else ((CTX, SEQ),)
                    for a, w in streams:
                        dve.scalar_tensor_tensor(out=out_[:, a + 1:a + w], in0=u[:, a:a + w - 1],
                                                 scalar=wt[:, VB_CW + n:VB_CW + n + 1], in1=out_[:, a + 1:a + w],
                                                 op0=ALU.mult, op1=ALU.add).then_inc(dchain, 1)
                        chain[0] += 1
                    dve.wait_ge(dchain, chain[0])
                    for a, w in streams:
                        ins = dve.scalar_tensor_tensor(out=out_[:, a:a + w - 1], in0=u[:, a + 1:a + w],
                                                       scalar=wt[:, VB_CW + 2 * KD + n:VB_CW + 2 * KD + n + 1],
                                                       in1=out_[:, a:a + w - 1], op0=ALU.mult, op1=ALU.add)
                    ins.then_inc(ctap_done, 1)
                    lo_after(QK_TILE + n)
                dve.wait_ge(rtr_done, 2 * l + 1)
                dve.tensor_copy(colF[:].rearrange("p a b -> p (a b)"), ps[:, 6, 0:NT * GROW]).then_inc(colF_done, 1)
                for i in range(O_TILE, WOUT_TILE):
                    lo_after(i)
                for z in range(2):
                    for n, (a, w) in enumerate(oh):
                        dve.wait_ge(sw_done, 4 * l + 2 * z + n + 1)
                        dve.wait_ge(feat_out, fb + 2 * (20 + z) + n + 1)
                        q = qrT[:, z, a:a + w]
                        link(dve.tensor_tensor(q, ps[:, 6 + n, 0:w], cosT[:, 1, a:a + w], ALU.mult))
                        link(dve.tensor_tensor(tmpq[:, 0:w], cv[z][:, a:a + w], cosT[:, 0, a:a + w], ALU.mult))
                        dve.tensor_tensor(q, q, tmpq[:, 0:w], ALU.add).then_inc(qr_out, 1)
                items = attn_items(l)
                a0 = items_before(l)
                for i in range(len(items) + 2):
                    if i < len(items):
                        h, tt = items[i]
                        dve.wait_ge(sc_done, a0 + i + 1)
                        b = 2 * (i % 2)
                        src = ps[:, b:b + 2, 0:HW] if tt >= NTC else ps[:, b, 0:CTX]
                        link(dve.tensor_reduce(stat[:, 0, i % 8:i % 8 + 1], src,
                                               AX.XY if tt >= NTC else AX.X, ALU.max))
                        dve.tensor_scalar(stat[:, 0, i % 8:i % 8 + 1], stat[:, 0, i % 8:i % 8 + 1], -SM_SCALE, None,
                                          ALU.mult).then_inc(max_done, 1)
                    if 1 <= i <= len(items) and items[i - 1][1] >= NTC:
                        h, tt = items[i - 1]
                        dve.wait_ge(pt_done, a0 + i)
                        if i - 1 >= 2:
                            dve.wait_ge(pv_done, a0 + i - 2)
                        dve.tensor_copy(ptb[:, (i - 1) % 2, 4:6].rearrange("p a b -> p (a b)"), ps[:, 5, 0:2 * P]
                                        ).then_inc(ptd_out, 1)
                    if i >= 2:
                        h, tt = items[i - 2]
                        k = (i - 2) % 8
                        dve.wait_ge(exp_done, a0 + i - 1)
                        link(dve.reciprocal(stat[:, 1, 8 + k:9 + k], stat[:, 1, k:k + 1]))
                        dve.wait_ge(pv_done, a0 + i - 1)
                        dve.tensor_scalar(atok[:, tt, h * VD:(h + 1) * VD], ps[:, 6 + (i - 2) % 2, 0:VD],
                                          stat[:, 1, 8 + k:9 + k], None, ALU.mult).then_inc(pv_out, 1)
                for h in range(MH + 1):
                    for j in range(NT if h < MH else 0):
                        for d in range(2):
                            diag, rest = source_blocks(l, d, j)
                            if diag is None:
                                continue
                            i = block_index(l, h, j, d)
                            s = slice(diag * P, (diag + 1) * P)
                            dve.wait_ge(g_out, 4 * (MH * l + h) + 2 * d + 2)
                            if i >= 2:
                                dve.wait_ge(pb_done, i - 1)
                            dve.scalar_tensor_tensor(
                                out=dbuf[:, d, s], in0=gbc[:, d, s],
                                scalar=colF[:, j, 32 * d + h:32 * d + h + 1],
                                in1=cst[:, C_MF + d * P:C_MF + (d + 1) * P], op0=ALU.add, op1=ALU.min
                            ).then_inc(dg_done, 1)
                        for d in range(2):
                            i = block_index(l, h, j, d)
                            dve.wait_ge(dx_done, i + 1)
                            dve.wait_ge(s_done, NT * (MH * l + h) + j + 1)
                            if h >= 2:
                                dve.wait_ge(mo_done, OUT_UNITS * l + 4 * (h - 1))
                            for slot, a, w in product_ranges(l, d, j):
                                src = ps[:, 4, j * CTX + a:j * CTX + a + w] if a < CTX else \
                                    ps[:, 2 + j % 2, a - CTX:a - CTX + w]
                                ins = dve.scalar_tensor_tensor(
                                    out=pblk[:, h % 2, d, slot:slot + w // P].rearrange("p a b -> p (a b)"),
                                    in0=src, scalar=K_SCALE, in1=dbuf[:, d, a:a + w], op0=ALU.mult, op1=ALU.mult)
                            ins.then_inc(pb_done, 1)
                    if h >= 1:
                        mlstm_out(l, h - 1)
                    if h == MH - 1:
                        normalise(l, range(MH - 1), True)
                normalise(l, [MH - 1], False)
                for n, (a, w) in enumerate(oh):
                    for cidx in range(KD):
                        i = 16 * l + KD * n + cidx
                        dve.wait_ge(mhi_done, i + 1)
                        dve.scalar_tensor_tensor(out=mixT[:, 1, cidx, a:a + w], in0=ps[:, i % 4, 0:w],
                                                 scalar=vecB[:, l, VB_AN + cidx:VB_AN + cidx + 1],
                                                 in1=mixT[:, 0, cidx, a:a + w].bitcast(F32),
                                                 op0=ALU.mult, op1=ALU.subtract).then_inc(mlo_done, 1)

            def normalise(l, heads, attn):
                tts = o_tts(l)
                t1, h1 = tts[0], heads[0]
                rs = stat[:, 2, 0:NT * MH].rearrange("p (h t) -> p h t", h=MH)[:, h1:heads[-1] + 1, t1:NT]
                var = mv[:, :, 1].rearrange("p (h t) -> p h t", h=MH)[:, h1:heads[-1] + 1, t1:NT]
                dve.tensor_copy(rs, var).then_inc(fvar_done, 1)
                dve.wait_ge(fstd_done, 3 * l + (2 if attn else 3))
                link(dve.reciprocal(rs, rs))
                if attn:
                    dve.reciprocal(stat[:, 3, t1:NT], stat[:, 3, t1:NT]).then_inc(frec_done, 1)
                for h in heads:
                    for tt in tts:
                        k = h * NT + tt
                        v = otok[:, tt, h * MDH:(h + 1) * MDH]
                        dve.tensor_scalar(v, v, mv[:, k, 0:1], stat[:, 2, k:k + 1], ALU.subtract, ALU.mult
                                          ).then_inc(fin_done, 1)

            def mlstm_out(l, h):
                for d in range(2):
                    for z, tts in enumerate(triples(l)):
                        o = OUT_UNITS * l + 4 * h + 2 * d + z
                        n = len(tts)
                        W = MDH + 1
                        bank = ps[:, 5 + o % 3, 0:n * W].rearrange("p (t e) -> p t e", e=W)
                        r = 32 * d + h
                        dve.wait_ge(mo_done, o + 1)
                        if o >= 1:
                            dve.wait_ge(mo_out, o)
                        link(dve.tensor_copy(dn[:, 1, 0:n], bank[:, :, MDH]))
                        link(dve.scalar_tensor_tensor(out=dn[:, 0, 0:n], in0=dn[:, 1, 0:n], scalar=-1.0,
                                                      in1=dn[:, 1, 0:n], op0=ALU.mult, op1=ALU.max))
                        link(dve.tensor_tensor(dn[:, 0, 0:n], dn[:, 0, 0:n], expnm[:, tts[0]:tts[0] + n, r],
                                               ALU.max))
                        link(dve.reciprocal(dn[:, 1, 0:n], dn[:, 0, 0:n]))
                        den = dn[:, 1, 0:n].unsqueeze(2).broadcast_to([P, n, MDH])
                        dst = hh[:, tts[0]:tts[0] + n]
                        if d == 0:
                            dve.tensor_tensor(dst, bank[:, :, 0:MDH], den, ALU.mult).then_inc(mo_out, 1)
                        else:
                            dve.tensor_tensor(ht[:, 0:n], bank[:, :, 0:MDH], den, ALU.mult).then_inc(mo_out, 1)
                            dve.wait_ge(mo_out, o + 1)
                            link(dve.tensor_tensor(dst, dst, ht[:, 0:n], ALU.add))
                tts = o_tts(l)
                g = otok[:, tts[0]:NT, h * MDH:(h + 1) * MDH]
                dve.wait_ge(o_outs, o_before(l) + len(tts))
                link(dve.tensor_tensor(g, g, hh[:, tts[0]:NT], ALU.mult))
                for i, tt in enumerate(tts):
                    link(dve.bn_stats(bn6[:, i % 2], otok[:, tt, h * MDH:(h + 1) * MDH]))
                    link(dve.bn_aggr(mv[:, h * NT + tt], bn6[:, i % 2]))

            link(dve.memset(epsc, EPS))
            link(dve.memset(onec, 1.0))
            dve.memset(zeroc, 0.0).then_inc(wlo_done, RAW)
            dve.memset(kc[:, 3:4], 0.0).then_inc(amul_done, 2)
            dve.wait_ge(amul_done, 2)
            dve.memset(kc[:, 3:4], 0.0).then_inc(yadd_done, 2)
            dve.wait_ge(yadd_done, 2)
            dve.memset(kc[:, 3:4], 0.0).then_inc(alo_done, 2)
            dve.wait_ge(alo_done, 2)
            dve.memset(kc[:, 3:4], 0.0).then_inc(mod_step, MOD_FREE)
            for i in range(2 * L):
                dve.wait_ge(vtr, i + 1)
                dve.tensor_copy((vecA if i % 2 else vecB)[:, i // 2], ps[:, 4 + i, 0:VA_N if i % 2 else VB_N]
                                ).then_inc(vev, 1)
                if i == 0:
                    for u in range(MOD0):
                        dve.wait_ge(mod_tr, u + 1)
                        dve.tensor_copy(modT[:, 4 * u:4 * u + 4],
                                        ps[:, 2 + u % 2, 0:8].rearrange("p (a b) -> p a b", b=2)).then_inc(mod_sum, 1)
            for i in range(2 * KD):
                dve.wait_ge(xtr, i + 1)
                n, k = i // KD, i % KD
                dve.tensor_copy(xT[:, k, n * HW:(n + 1) * HW], ps[:, i % 6, 0:HW]).then_inc(xev, 1)
            columns(0, 0, 0)
            columns(0, 0, 1)
            for l in range(L):
                for sub in range(3):
                    steps(lead_steps(l, sub), (l, sub - 1) if sub else (l - 1, 2), (l, sub))
                    if sub == 1:
                        mixer(l)
                    else:
                        ffn(l, sub // 2)
                    columns(l, sub, 2)
                    if has_next(after(l, sub)):
                        columns(*after(l, sub), 0)
                        columns(*after(l, sub), 1)
                    last_pass(l, sub)
                    steps(tail_steps(l, sub), (l, sub), after(l, sub))

        @block.tensor
        def _(pe):
            def three(dst, w, x, first, last):
                pe.matmul(dst, w(0), x(0), start=first, stop=False)
                pe.matmul(dst, w(0), x(1), start=False, stop=False)
                return pe.matmul(dst, w(1), x(0), start=False, stop=last)

            def weight(cs, at, width=P):
                return lambda p: wsp[:, cs, p, at:at + width]

            def mean(l, sub, post, n):
                w = halves_of(l, sub, post)[n][1]
                e = MEAN_AT[l, sub, post, n]
                if e >= 2:
                    pe.wait_ge(rstd_done, e - 1)
                pe.wait_ge(acc_done, SQ_AT[l, sub, post, n, KD - 1] + 1)
                pe.matmul(ps[:, 6 + e % 2, 0:w], ones, acc[post][:, 0:w], start=True, stop=True).then_inc(stat_mm, 1)

            def mod_first(u):
                if u >= 2:
                    pe.wait_ge(mod0_out, u - 1)
                for j in range(4):
                    m = 4 * u + j
                    pe.wait_ge(mod0_in[m % MODR0], 16 * (m // MODR0 + 1))
                    for kk in range(2):
                        ins = pe.matmul(ps[0:2, u % 2], silc[:, :, 2 * j + kk], modw0[:, m % MODR0, kk],
                                        start=j == 0 and kk == 0, stop=j == 3 and kk == 1)
                    ins.then_inc(mod0_used, 1)

            def mod0_turn(u):
                pe.wait_ge(mod0_out, u + 1)
                if u >= 2:
                    pe.wait_ge(mod_sum, u - 1)
                for b in range(4):
                    ins = pe.transpose(ps[:, 2 + u % 2, 2 * b:2 * b + 2], macc[0:2, u % 2, b * P:(b + 1) * P],
                                       ident[0:2, 0:2])
                ins.then_inc(mod_tr, 1)

            def mod_turn(u):
                pe.wait_ge(mod_step, 16 * (u - MOD0) + 16 + MOD_FREE)
                pe.wait_ge(mod_sum, u)
                for v in range(2):
                    for b in range(4):
                        ins = pe.transpose(ps[:, 6 + v, b * P:(b + 1) * P], macc[:, v, b * P:(b + 1) * P], ident)
                ins.then_inc(mod_tr, 1)

            def output(bank, cs, G, a, w, x, ready=None):
                for k in range(G):
                    if ready is not None:
                        ready(k)
                    ins = three(ps[:, bank, 0:w], weight(cs, k * P), lambda p: x[:, p, k, a:a + w],
                                k == 0, k == G - 1)
                ins.then_inc(unit_done, 1)

            def last_output(l, sub, n, dt, s, ready=None):
                a, w = halves_of(l, sub, 1)[n]
                pe.wait_ge(wlo_done, last_tile0(l, sub) + KD * n + dt + 1 + RAW)
                pe.wait_ge(yadd_done, last_down0(l, sub) + KD * n + dt + 1)
                output(4 + s % 2, s % 2, last_width(l, sub) // P, a, w, mixT if sub == 1 else aT, ready)

            def last_pass(l, sub):
                if sub == 1:
                    for dt in range(KD):
                        last_output(l, sub, 0, dt, dt, None if dt else
                                    lambda k: pe.wait_ge(mlo_done, 16 * l + k + 1))
                    pe.wait_ge(mlo_done, 16 * (l + 1))
                    return
                pe.wait_ge(alo_done, ffn_pair0(l, sub // 2) + 2 * NCH + 2)
                pe.wait_ge(pad_done, 2 * l + sub // 2 + 1)
                with pe.Fori(0, KD // 4) as i:
                    for s in range(4):
                        last_output(l, sub, 0, 4 * i + s, s)

            def head(l, sub, n, k, ready):
                t = first_tile0(l, sub) + HEAD * n + k
                a, w = halves_of(l, sub, 0)[n]
                pe.wait_ge(wlo_done, t + 1 + RAW)
                output(HEAD_BANKS[n][k], t % 2, KD, a, w, hn, ready)

            def input_ready(l, sub, n):
                return lambda k: pe.wait_ge(hlo_done, KD * pre_event(l, sub, n) + k + 1)

            def steps(which, prev, cur):
                for kind, post, n, k in which:
                    if kind == "down":
                        last_output(*prev, 1, k, k)
                    if kind == "head":
                        if k == 0:
                            pe.wait_ge(yadd_done, (last_down0(*prev) + DOWN_OUT if cur != (0, 0) else 0) + 2)
                        head(*cur, 0, k, input_ready(*cur, 0) if k == 0 else None)
                    if kind == "mean":
                        mean(*(prev if post else cur), post, n)

            def ffn(l, j):
                t0, q0, d0 = ffn_tile0(l, j), ffn_pair0(l, j), ffn_down0(l, j)
                hv = halves_of(l, 2 * j, 1)
                assert hv == halves_of(l, 2 * j, 0)
                for k in range(HEAD):
                    if k >= 2:
                        pe.wait_ge(silu_done if k == 2 else amul_done, q0 + 3)
                    head(l, 2 * j, 1, k, input_ready(l, 2 * j, 1) if k == 0 else None)
                t0 += 2 * HEAD
                q0 += HEAD
                for g, (c0, G) in enumerate(GROUPS):
                    def up_body(i, first, mod):
                        for b in range(2):
                            t = t0 + 4 * i + 2 * b
                            q = q0 + 4 * i + 2 * b
                            for wi, freed in ((0, silu_done), (1, amul_done)):
                                pe.wait_ge(wlo_done, t + wi + 1 + RAW)
                                for n, (a, w) in enumerate(hv):
                                    pe.wait_ge(freed, q + 1 + max(n, first))
                                    output(2 * wi + n, wi, KD, a, w, hn)
                        if mod is not None:
                            mod_turn(mod[0] + i)

                    k0, n_loop = up_loop(g)
                    mod = mod_plan(l, j, g, UP)
                    first = 1 if g == 0 else 0
                    with pe.Fori(0, n_loop) as i:
                        up_body(i, first, mod)
                    if g == len(GROUPS) - 1:
                        last_mod = mod_plan(l, j, g, UP_LAST)
                        up_body(n_loop, first, last_mod and (last_mod[0] - n_loop, 1))
                        return
                    t0 += 2 * (G - k0)
                    q0 += 2 * (G - k0)
                    mod = mod_plan(l, j, g, DOWN)
                    with pe.Fori(0, KD // 4) as i:
                        for s in range(4):
                            pe.wait_ge(wlo_done, t0 + 4 * i + s + 1 + RAW)
                            for n, (a, w) in enumerate(hv):
                                pe.wait_ge(yadd_done, d0 + 8 * i + 2 * s + n + 1)
                                if s == 0 and n == 0:
                                    pe.wait_ge(alo_done, q0 + 2)
                                output(4 + n, s % 2, G, a, w, aT)
                        if mod is not None:
                            mod_turn(mod[0] + i)
                    t0 += KD
                    d0 += DOWN_OUT

            def mixer(l):
                t0 = mix_tile0(l)
                fb = 2 * N_FEAT * l
                fh, oh = full_halves(l), out_halves(l)

                def split(i):
                    pe.wait_ge(wlo_done, t0 + i + 1 + RAW)
                    return (t0 + i) % 2

                def feature(f, cs, K, wat, x, halves, step=P):
                    for n, (a, w) in enumerate(halves):
                        for k in range(K):
                            ins = three(ps[:, 2 * (f % 2) + n, 0:w], weight(cs, wat + k * step),
                                        lambda p: x(p, k, a, w), k == 0, k == K - 1)
                        ins.then_inc(unit_done, 1)

                def normed(p, k, a, w):
                    return hn[:, p, k, a:a + w]

                def small(z, lhsT, rhs, halves, rows_=P):
                    for n, (a, w) in enumerate(halves):
                        pe.matmul(ps[0:rows_, 6 + n, 0:w], lhsT, rhs[:, a:a + w], start=True, stop=True
                                  ).then_inc(sel_done, 1)

                def lat_stat(i, src, halves, first, last):
                    for n, (a, w) in enumerate(halves):
                        pe.wait_ge(lsq_done, 6 * l + 2 * i + n + 1)
                        pe.matmul(ps[:, 6 + n, 0:w], ones, sq2[n][:, 0:w], start=first, stop=last
                                  ).then_inc(lstat_done, 1)

                def token_major(i, j, tts, width, freed):
                    cs = split(i)
                    for tt in tts:
                        if j == 0:
                            freed(tt)
                        for k in range(2):
                            ins = three(ps[:, tt, 0:width], lambda p: hn[:, p, 2 * j + k, tt * P:(tt + 1) * P],
                                        lambda p: wsp[:, cs, p, k * MW:(k + 1) * MW], j == 0 and k == 0,
                                        j == 3 and k == 1)
                        if j == 3 or tt == tts[-1]:
                            ins.then_inc(unit_done, 1)

                head(l, 1, 1, 0, input_ready(l, 1, 1))
                head(l, 1, 1, 1, None)
                pe.wait_ge(feat_out, fb + feat_seq(0, 1) + 1)
                pe.wait_ge(rstd_done, MEAN_AT[l, 1, 0, 1] + 1)
                small(0, cst[:, C_SELI:C_SELI + GROW], krg, fh, GROW)
                pe.wait_ge(feat_out, fb + 1)
                head(l, 1, 1, 2, None)
                pe.wait_ge(gates_out, 4 * l + 2)
                small(1, cst[:, C_SELF:C_SELF + GROW], krg, fh, GROW)
                pe.wait_ge(feat_out, fb + 2)
                head(l, 1, 1, 3, None)
                pe.wait_ge(gates_out, 4 * l + 4)
                small(2, cst[:, C_KD:C_KD + P], krg, fh)

                def v_free(tt):
                    pe.wait_ge(feat_out, fb + 2 * HEAD)

                token_major(V_TILE, 0, range(NT), MW, v_free)
                pe.wait_ge(kro_out, 4 * l + 2)
                small(3, cst[:, C_KSW:C_KSW + P], krg, fh)
                pe.wait_ge(kro_out, 4 * l + 4)
                lat_stat(0, ckv, fh, True, True)
                token_major(V_TILE + 1, 1, range(NT), MW, None)
                pe.wait_ge(lstd_done, 4 * l + 2)
                lat_stat(1, cq[:, 0], oh, True, False)
                lat_stat(2, cq[:, 1], oh, False, True)
                token_major(V_TILE + 2, 2, range(NT), MW, None)
                token_major(V_TILE + 3, 3, range(NT), MW, None)
                for n in range(KD):
                    f = 4 + n
                    cs = split(QK_TILE + n)
                    if n < 2:
                        pe.wait_ge(v_out, NT * l + 2 * (n + 1))
                    else:
                        pe.wait_ge(feat_out, fb + 2 * (f - 1))
                    feature(f, cs, KD, 0, normed, oh if n < MH else fh)
                    if n == 4:
                        pe.wait_ge(rows_done, l + 1)
                        pe.wait_ge(lstd_done, 4 * l + 4)
                        for src, bank in ((rI, 6), (rB, 7)):
                            for tt in range(NT):
                                ins = pe.transpose(ps[:, bank, tt * GROW:(tt + 1) * GROW], src[:, tt * P:(tt + 1) * P],
                                                   ident[0:GROW, 0:GROW])
                            ins.then_inc(rtr_done, 1)

                def o_free(tt):
                    pe.wait_ge(feat_out, fb + 24)
                    pe.wait_ge(v_out, NT * (l + 1))

                for j in range(4):
                    token_major(O_TILE + j, j, o_tts(l), MW, o_free)
                pe.wait_ge(lat_done, 6 * (l + 1))
                cs = split(UKN_TILE)
                for h in range(HEADS):
                    if h == 0:
                        pe.wait_ge(o_outs, o_before(l) + len(o_tts(l)))
                    else:
                        pe.wait_ge(feat_out, fb + 2 * (12 + h - 1))
                    feature(12 + h, cs, 1, h * P, lambda p, k, a, w: ckn[:, p, a:a + w], fh)
                cs = split(UVA_TILE)
                pe.wait_ge(feat_out, fb + 32)
                for tt in range(NT):
                    three(ps[:, tt], lambda p: ckn[:, p, tt * P:(tt + 1) * P], weight(cs, 0, HEADS * P), True, True
                          ).then_inc(unit_done, 1)
                cs = split(UQN_TILE)
                for h in range(HEADS):
                    if h < 2:
                        pe.wait_ge(va_out, NT * l + 2 * (h + 1))
                    else:
                        pe.wait_ge(feat_out, fb + 2 * (16 + h - 1))
                    feature(16 + h, cs, 2, h * P, lambda p, k, a, w: cqn[:, p, k, a:a + w], oh, HEADS * NOPE)
                cs = split(UQR_TILE)
                for z in range(2):
                    pe.wait_ge(feat_out, fb + 2 * (20 + z - 1))
                    feature(20 + z, cs, 2, z * P, lambda p, k, a, w: cqn[:, p, k, a:a + w], oh, HEADS * ROPE)
                pe.wait_ge(colF_done, l + 1)
                pe.wait_ge(expnm_done, l + 1)
                for z in range(2):
                    for n, (a, w) in enumerate(oh):
                        pe.wait_ge(feat_out, fb + 2 * (20 + z) + n + 1)
                        if z == 1:
                            pe.wait_ge(qr_out, 4 * l + n + 1)
                        pe.matmul(ps[:, 6 + n, 0:w], cst[:, C_SWQ:C_SWQ + P], cv[z][:, a:a + w], start=True, stop=True
                                  ).then_inc(sw_done, 1)
                items = attn_items(l)
                a0 = items_before(l)
                pe.wait_ge(va_out, NT * (l + 1))

                def scores(i):
                    h, tt = items[i]
                    if i >= 2:
                        pe.wait_ge(exp_done, a0 + i - 1)
                    q = 64 * (h % 2)
                    for b in range(2 if tt >= NTC else 1):
                        ks = slice(b * HW, (b + 1) * HW) if tt >= NTC else slice(0, CTX)
                        dst = ps[:, 2 * (i % 2) + b, 0:ks.stop - ks.start]
                        pe.matmul(dst, qnT[:, h, tt * P:(tt + 1) * P], knT[:, h, ks], start=True, stop=False)
                        ins = pe.matmul(dst, qrT[q:q + 64, h // 2, tt * P:(tt + 1) * P], krT[q:q + 64, ks],
                                        start=False, stop=True)
                    ins.then_inc(sc_done, 1)

                def turn(i):
                    h, tt = items[i]
                    pe.wait_ge(exp_done, a0 + i + 1)
                    if i >= 1:
                        pe.wait_ge(pta_out, a0 + i)
                        if turned_by_dve(l, i - 1) > 0:
                            pe.wait_ge(ptd_out, turned_by_dve(l, i - 1))
                    for s in range(NT if tt >= NTC else NTC):
                        ins = pe.transpose(ps[:, 4 + s // 4, (s % 4) * P:(s % 4 + 1) * P],
                                           pbuf[:, i % 2, s * P:(s + 1) * P], ident)
                    ins.then_inc(pt_done, 1)

                def values(i):
                    h, tt = items[i]
                    pe.wait_ge(pta_out, a0 + i + 1)
                    if tt >= NTC:
                        pe.wait_ge(ptd_out, turned_by_dve(l, i))
                    if i >= 2:
                        pe.wait_ge(pv_out, a0 + i - 1)
                    ns = NT if tt >= NTC else NTC
                    for s in range(ns):
                        ins = pe.matmul(ps[:, 6 + i % 2, 0:VD], ptb[:, i % 2, s], va[:, s, h * VD:(h + 1) * VD],
                                        start=s == 0, stop=s == ns - 1)
                    ins.then_inc(pv_done, 1)

                pe.wait_ge(qr_out, 4 * (l + 1))
                scores(0)
                for i in range(len(items) + 1):
                    if i + 1 < len(items):
                        scores(i + 1)
                    if i < len(items):
                        turn(i)
                    if i >= 1:
                        values(i - 1)
                pe.wait_ge(ones_done, l + 1)

                def head_scores(h):
                    for d in range(2):
                        for z, (a, w) in enumerate(((0, CTX), (CTX, SEQ))):
                            gi = 4 * (MH * l + h) + 2 * d + z
                            if gi >= 2:
                                pe.wait_ge(g_out, gi - 1)
                            row = 32 * d + h
                            pe.matmul(ps[:, z, 0:w], ident[0:GROW, row:row + 1].broadcast_to([GROW, P]), negG[0:GROW, a:a + w],
                                      start=True, stop=True).then_inc(g_done, 1)
                    for j in range(NT):
                        if h > 0 or j >= 2:
                            pe.wait_ge(pb_done, block_index(l, h, j, 0) - 2)
                        if j == 0 and l < L - 1:
                            for jj in range(NTC):
                                pe.matmul(ps[:, 4, jj * CTX:(jj + 1) * CTX], qkT[:, MH + h, jj * P:(jj + 1) * P],
                                          qkT[:, h, 0:CTX], start=True, stop=True)
                        pe.matmul(ps[:, 2 + j % 2, 0:SEQ], qkT[:, MH + h, j * P:(j + 1) * P], qkT[:, h, CTX:T],
                                  start=True, stop=True).then_inc(s_done, 1)

                def head_out(h):
                    for d in range(2):
                        slots = source_slots(l, d)
                        for z, tts in enumerate(triples(l)):
                            o = OUT_UNITS * l + 4 * h + 2 * d + z
                            if o >= 3:
                                pe.wait_ge(mo_out, o - 2)
                            pe.wait_ge(pb_done, block_index(l, h, NT, 0))
                            for m, tt in enumerate(tts):
                                dst = ps[:, 5 + o % 3, m * (MDH + 1):(m + 1) * (MDH + 1)]
                                src = sources_of(d, tt)
                                for j in src:
                                    ins = pe.matmul(dst, pblk[:, h % 2, d, slots[j, tt]], vext[:, j, h],
                                                    start=j == src[0], stop=j == src[-1])
                            ins.then_inc(mo_done, 1)

                pe.wait_ge(conv_done, KD * (l + 1))
                pe.wait_ge(pv_out, a0 + len(items))
                head_scores(0)
                for h in range(MH):
                    if h + 1 < MH:
                        head_scores(h + 1)
                    head_out(h)
                tts = o_tts(l)
                for n, (a, w) in enumerate(oh):
                    for cidx in range(KD):
                        i = 16 * l + KD * n + cidx
                        if cidx < HEADS:
                            pe.wait_ge(afin_done, (NT if l else 0) + len(tts))
                        else:
                            pe.wait_ge(fin_done, fin_before(l) + len(tts) * (cidx - HEADS + 1))
                        if i >= 4:
                            pe.wait_ge(mlo_done, i - 3)
                        src = atok if cidx < HEADS else otok
                        at = (cidx % HEADS) * P
                        for m in range(w // P):
                            ins = pe.transpose(ps[:, i % 4, m * P:(m + 1) * P], src[:, a // P + m, at:at + P], ident)
                        ins.then_inc(mt_done, 1)

            pe.wait_ge(cst_in, 16)

            def turn_rows(i):
                n = VA_N if i % 2 else VB_N
                pe.transpose(ps[:, 4 + i, 0:n], vstage[0:n, i], ident[0:n, 0:n]).then_inc(vtr, 1)

            pe.wait_ge(cvec_in, 16 * 8)
            turn_rows(0)
            pe.wait_ge(silu_done, 2)
            for u in range(MOD0):
                mod_first(u)
                if u >= 1:
                    mod0_turn(u - 1)
            mod0_turn(MOD0 - 1)
            pe.wait_ge(vec_in, 16 * (11 * L - 8))
            for i in range(1, 2 * L):
                turn_rows(i)
            pe.wait_ge(x_in, 32)
            pe.wait_ge(vev, 2 * L)
            pe.wait_ge(mod_sum, MOD0)
            for i in range(2 * KD):
                if i >= 6:
                    pe.wait_ge(xev, i - 5)
                n, k = i // KD, i % KD
                for m in range(3):
                    ins = pe.transpose(ps[:, i % 6, m * P:(m + 1) * P], xstage[:, 3 * n + m, k * P:(k + 1) * P], ident)
                ins.then_inc(xtr, 1)
            pe.wait_ge(xev, 2 * KD)
            for l in range(L):
                for sub in range(3):
                    steps(lead_steps(l, sub), (l, sub - 1) if sub else (l - 1, 2), (l, sub))
                    if sub == 1:
                        mixer(l)
                    else:
                        ffn(l, sub // 2)
                    last_pass(l, sub)
                    steps(tail_steps(l, sub), (l, sub), after(l, sub))
            for i in range(2 * (SEQ // P)):
                tt, half = NTC + i // 2, i % 2
                pe.wait_ge(x_done, KD * (post_event(L - 1, 2, i // SEQ_TILES) + 1))
                if i >= 4:
                    pe.wait_ge(oev, i - 3)
                for m in range(4):
                    ins = pe.transpose(ps[:, i % 4, m * P:(m + 1) * P], xT[:, 4 * half + m, tt * P:(tt + 1) * P], ident)
                ins.then_inc(otr, 1)


_INS = ["x", "c", "ctx", "c_ctx", "w_mod", "b_mod", "norm_pre", "norm_post", "ffn_w_gate", "ffn_w_up", "ffn_w_down",
        "w_in", "q_norm", "w_uq", "kv_norm", "w_ukv", "attn_out_norm", "conv_w", "conv_b", "gate_b", "mlstm_norm",
        "w_out"]


def kernel(**inputs):
    import concourse.bacc as bacc
    from concourse.bass_utils import run_bass_kernel_spmd

    nc = bacc.Bacc("TRN2", target_bir_lowering=False, num_devices=1)
    arrays, args = {}, []
    for name in _INS:
        a = np.ascontiguousarray(inputs[name])
        arrays[f"in_{name}"] = a
        args.append(nc.dram_tensor(f"in_{name}", a.shape, mybir.dt.from_np(a.dtype), kind="ExternalInput").ap())
    arrays["in_consts"] = constants()
    args.append(nc.dram_tensor("in_consts", (P, C_N), F32, kind="ExternalInput").ap())
    args.append(nc.dram_tensor("out", (1, SEQ, D), F32, kind="ExternalOutput").ap())
    hybrid_backbone_kernel(nc, *args)
    r = run_bass_kernel_spmd(nc, [arrays], core_ids=[0])
    return r.results[0]["out"]
```
